# Optimizing a Trainium2 kernel written in Bass

```python
import jax, jax.numpy as jnp
from jax import lax
import numpy as np
import math

D_MODEL = 1024
BATCH = 1
SEQ = 512
DEPTH = 1

CHUNK = 64
EPS = 1e-6
N_BRANCH = 2
CONV_DIM = D_MODEL
CONV_WIDTH = 3
SSM_EXPAND = 2
D_SSM = SSM_EXPAND * D_MODEL
SSM_HEAD_DIM = 64
SSM_HEADS = D_SSM // SSM_HEAD_DIM
SSM_GROUPS = 8
SSM_STATE = 128
SSM_CONV_WIDTH = 4
SSM_CONV_DIM = D_SSM + 2 * SSM_GROUPS * SSM_STATE
DT_MIN = 1e-3
DT_MAX = 1e-1
D_FF = 4 * D_MODEL
N_MOD = 6


def proj_sizes():
    return (N_BRANCH * D_MODEL,
            CONV_DIM, CONV_DIM, CONV_DIM,
            D_SSM,
            SSM_CONV_DIM,
            SSM_HEADS)

def rms_norm(x, w):
    xf = x.astype(jnp.float32)
    y = xf * lax.rsqrt(jnp.mean(xf * xf, axis=-1, keepdims=True) + EPS)
    return (y * w.astype(jnp.float32)).astype(x.dtype)

def causal_depthwise_conv(x, w):
    k = w.shape[0]
    return lax.conv_general_dilated(
        x, w[:, None, :].astype(x.dtype), window_strides=(1,), padding=((k - 1, 0),),
        dimension_numbers=('NWC', 'WIO', 'NWC'), feature_group_count=x.shape[-1])

def ssd_scan(x, a, b, c):
    bsz, seqlen, h, p = x.shape
    g, n = b.shape[-2:]
    r = h // g
    nc = seqlen // CHUNK

    def to_chunks(t):
        return jnp.moveaxis(t.reshape(bsz, nc, CHUNK, *t.shape[2:]), 1, 0)

    xs = (to_chunks(x.reshape(bsz, seqlen, g, r, p)),
          to_chunks(a.reshape(bsz, seqlen, g, r)),
          to_chunks(b), to_chunks(c))
    tril = jnp.tril(jnp.ones((CHUNK, CHUNK), dtype=bool))[None, :, :, None, None]

    def step(state, inp):
        xq, aq, bq, cq = inp
        a_cum = jnp.cumsum(aq, axis=1)
        seg = a_cum[:, :, None] - a_cum[:, None, :]
        decay = jnp.exp(jnp.where(tril, seg, -jnp.inf))
        scores = jnp.einsum('btgn,bsgn->btsg', cq, bq)
        y_diag = jnp.einsum('btsg,btsgr,bsgrp->btgrp', scores, decay, xq)
        y_off = jnp.einsum('btgn,bgrpn->btgrp', cq, state) * jnp.exp(a_cum)[..., None]
        to_end = jnp.exp(a_cum[:, -1:] - a_cum)
        new_state = (state * jnp.exp(a_cum[:, -1])[..., None, None]
                     + jnp.einsum('bsgn,bsgr,bsgrp->bgrpn', bq, to_end, xq))
        return new_state, y_diag + y_off

    state0 = jnp.zeros((bsz, g, r, p, n), jnp.float32)
    _, y = lax.scan(step, state0, xs)
    return jnp.moveaxis(y, 0, 1).reshape(bsz, seqlen, h, p)

def mixer_sublayer(u, w_in, conv_w, ssm_conv_w, ssm_conv_b, dt_bias, a_log, d_skip,
                   ssm_norm_w, w_conv_out, w_ssm_out, w_o):
    bsz, seqlen, _ = u.shape
    proj = u @ w_in
    split_at = [int(v) for v in np.cumsum(proj_sizes())[:-1]]
    gl, cb, cc, cx, z, xbc, dt = jnp.split(proj, split_at, axis=-1)

    y_conv = cb * causal_depthwise_conv(cc * cx, conv_w)
    p_conv = y_conv @ w_conv_out

    xbc = jax.nn.silu(causal_depthwise_conv(xbc, ssm_conv_w) + ssm_conv_b.astype(xbc.dtype))
    xbc = xbc.astype(jnp.float32)
    xs, bs, cs = jnp.split(xbc, [D_SSM, D_SSM + SSM_GROUPS * SSM_STATE], axis=-1)
    xs = xs.reshape(bsz, seqlen, SSM_HEADS, SSM_HEAD_DIM)
    bs = bs.reshape(bsz, seqlen, SSM_GROUPS, SSM_STATE)
    cs = cs.reshape(bsz, seqlen, SSM_GROUPS, SSM_STATE)
    dt = jax.nn.softplus(dt.astype(jnp.float32) + dt_bias.astype(jnp.float32))
    a = -jnp.exp(a_log.astype(jnp.float32))
    y = ssd_scan(xs * dt[..., None], dt * a, bs, cs)
    y = y + d_skip.astype(jnp.float32)[:, None] * xs
    y = y.reshape(bsz, seqlen, D_SSM) * jax.nn.silu(z.astype(jnp.float32))
    yg = y.reshape(bsz, seqlen, SSM_GROUPS, D_SSM // SSM_GROUPS)
    yg = yg * lax.rsqrt(jnp.mean(yg * yg, axis=-1, keepdims=True) + EPS)
    y = (yg.reshape(bsz, seqlen, D_SSM) * ssm_norm_w.astype(jnp.float32)).astype(u.dtype)
    p_ssm = y @ w_ssm_out

    g_conv, g_ssm = jnp.split(jax.nn.sigmoid(gl), 2, axis=-1)
    merged = g_conv * p_conv + g_ssm * p_ssm
    return merged @ w_o

def first_inputs(seed: int = 0) -> dict:
    key = jax.random.key(seed)
    ks = jax.random.split(key, 24)
    d_proj = sum(proj_sizes())
    f32 = jnp.float32

    def nrm(k, shape, scale):
        return jax.random.normal(k, shape, f32) * scale

    dt0 = jnp.exp(jax.random.uniform(ks[10], (DEPTH, SSM_HEADS), f32,
                                     np.log(DT_MIN), np.log(DT_MAX)))
    dt_bias = dt0 + jnp.log(-jnp.expm1(-dt0))
    return {
        "x": nrm(ks[0], (BATCH, SEQ, D_MODEL), 1.0),
        "c": nrm(ks[1], (BATCH, D_MODEL), 1.0),
        "w_ada": nrm(ks[2], (DEPTH, D_MODEL, N_MOD * D_MODEL), 0.5 * D_MODEL ** -0.5),
        "b_ada": nrm(ks[3], (DEPTH, N_MOD * D_MODEL), 0.02),
        "ln1": 1.0 + nrm(ks[4], (DEPTH, D_MODEL), 0.1),
        "ln2": 1.0 + nrm(ks[5], (DEPTH, D_MODEL), 0.1),
        "w_in": nrm(ks[6], (DEPTH, D_MODEL, d_proj), D_MODEL ** -0.5),
        "conv_w": nrm(ks[7], (DEPTH, CONV_WIDTH, CONV_DIM), CONV_WIDTH ** -0.5),
        "ssm_conv_w": nrm(ks[8], (DEPTH, SSM_CONV_WIDTH, SSM_CONV_DIM), SSM_CONV_WIDTH ** -0.5),
        "ssm_conv_b": nrm(ks[9], (DEPTH, SSM_CONV_DIM), 0.01),
        "dt_bias": dt_bias,
        "a_log": jnp.log(jax.random.uniform(ks[11], (DEPTH, SSM_HEADS), f32, 1.0, 16.0)),
        "d_skip": 1.0 + nrm(ks[12], (DEPTH, SSM_HEADS), 0.1),
        "ssm_norm_w": 1.0 + nrm(ks[13], (DEPTH, D_SSM), 0.1),
        "w_conv_out": nrm(ks[14], (DEPTH, CONV_DIM, D_MODEL), CONV_DIM ** -0.5),
        "w_ssm_out": nrm(ks[15], (DEPTH, D_SSM, D_MODEL), D_SSM ** -0.5),
        "w_o": nrm(ks[16], (DEPTH, D_MODEL, D_MODEL), D_MODEL ** -0.5),
        "w_up": nrm(ks[17], (DEPTH, D_MODEL, D_FF), D_MODEL ** -0.5),
        "w_down": nrm(ks[18], (DEPTH, D_FF, D_MODEL), D_FF ** -0.5),
        "final_norm": 1.0 + nrm(ks[19], (D_MODEL,), 0.1),
    }

def first_block(x, c, w_ada, b_ada, ln1, ln2, w_in, conv_w, ssm_conv_w, ssm_conv_b,
              dt_bias, a_log, d_skip, ssm_norm_w, w_conv_out, w_ssm_out, w_o,
              w_up, w_down, final_norm):
    bsz = x.shape[0]
    c_act = jax.nn.silu(c)
    for i in range(DEPTH):
        mod = (c_act @ w_ada[i] + b_ada[i]).reshape(bsz, N_MOD, D_MODEL)[:, :, None, :]
        shift1, scale1, gate1 = mod[:, 0], mod[:, 1], mod[:, 2]
        shift2, scale2, gate2 = mod[:, 3], mod[:, 4], mod[:, 5]

        u = rms_norm(x, ln1[i]) * (1.0 + scale1) + shift1
        mix = mixer_sublayer(u, w_in[i], conv_w[i], ssm_conv_w[i], ssm_conv_b[i], dt_bias[i],
                             a_log[i], d_skip[i], ssm_norm_w[i], w_conv_out[i],
                             w_ssm_out[i], w_o[i])
        x = x + gate1 * mix

        u2 = rms_norm(x, ln2[i]) * (1.0 + scale2) + shift2
        hid = jnp.square(jax.nn.relu(u2 @ w_up[i]))
        x = x + gate2 * (hid @ w_down[i])
    return rms_norm(x, final_norm)


N_HEADS_A = 8
HEAD_DIM_A = 64
N_IDX_HEADS = 16
IDX_DIM = 64
TOPK_MAX = 256
N_HEADS_B = 8
QK_NOPE_DIM = 64
QK_ROPE_DIM = 32
V_DIM_B = 64
Q_LORA = 384
KV_LORA = 256
D_MIX = N_HEADS_A * HEAD_DIM_A + N_HEADS_B * V_DIM_B
D_FF_2 = 2816
ROPE_THETA = 10000.0
Q_BLOCK = 128

PROJ_SIZES = (
    N_HEADS_A * HEAD_DIM_A,
    HEAD_DIM_A,
    HEAD_DIM_A,
    N_IDX_HEADS * IDX_DIM,
    IDX_DIM,
    N_IDX_HEADS,
    Q_LORA,
    KV_LORA,
    QK_ROPE_DIM,
)
D_PROJ = sum(PROJ_SIZES)


def rmsnorm(x, g):
    xf = x.astype(jnp.float32)
    y = xf * lax.rsqrt(jnp.mean(xf * xf, axis=-1, keepdims=True) + EPS)
    return (y * g.astype(jnp.float32)).astype(x.dtype)

def swiglu(x, w_gate, w_up, w_down):
    return (jax.nn.silu(x @ w_gate) * (x @ w_up)) @ w_down

def rope_tables(seq_len, dim):
    pos = jnp.arange(seq_len, dtype=jnp.float32)
    inv_freq = ROPE_THETA ** (-jnp.arange(0, dim, 2, dtype=jnp.float32) / dim)
    ang = pos[:, None] * inv_freq[None, :]
    return jnp.cos(ang), jnp.sin(ang)

def apply_rope(x, cos, sin):
    shape = (cos.shape[0],) + (1,) * (x.ndim - 3) + (cos.shape[1],)
    c = cos.reshape(shape)
    s = sin.reshape(shape)
    xf = x.astype(jnp.float32)
    x1, x2 = jnp.split(xf, 2, axis=-1)
    return jnp.concatenate([x1 * c - x2 * s, x1 * s + x2 * c], axis=-1).astype(x.dtype)

def block_slice(a, start):
    return lax.dynamic_slice_in_dim(a, start, Q_BLOCK, axis=1)

def dsa_sparse_attention(q, k, v, q_idx, k_idx, w_idx):
    B, T = q.shape[0], q.shape[1]
    top_k = min(TOPK_MAX, T // 4)
    n_blocks = T // Q_BLOCK
    key_pos = jnp.arange(T)
    scale = HEAD_DIM_A ** -0.5
    idx_scale = (N_IDX_HEADS * IDX_DIM) ** -0.5

    def one_block(i):
        s0 = i * Q_BLOCK
        qb = block_slice(q, s0)
        qib = block_slice(q_idx, s0)
        wb = block_slice(w_idx, s0).astype(jnp.float32) * idx_scale
        qpos = s0 + jnp.arange(Q_BLOCK)
        causal = key_pos[None, :] <= qpos[:, None]
        idx_logits = jnp.einsum('bqhd,bsd->bqhs', qib, k_idx).astype(jnp.float32)
        score = jnp.einsum('bqh,bqhs->bqs', wb, jax.nn.relu(idx_logits))
        score = jnp.where(causal[None], score, -jnp.inf)
        _, sel = lax.top_k(score, top_k)
        valid = sel <= qpos[None, :, None]
        kg = jax.vmap(lambda kb, ib: kb[ib])(k, sel)
        vg = jax.vmap(lambda vb, ib: vb[ib])(v, sel)
        att = jnp.einsum('bqhd,bqkd->bqhk', qb, kg).astype(jnp.float32) * scale
        att = jnp.where(valid[:, :, None, :], att, -jnp.inf)
        p = jax.nn.softmax(att, axis=-1)
        return jnp.einsum('bqhk,bqkd->bqhd', p.astype(vg.dtype), vg)

    out = lax.map(one_block, jnp.arange(n_blocks))
    return jnp.moveaxis(out, 0, 1).reshape(B, T, N_HEADS_A * HEAD_DIM_A)

def mla_attention(c_q, c_kv, k_rope, g_q_lat, g_kv_lat, w_uq, w_ukv, cos_b, sin_b):
    B, T = c_q.shape[0], c_q.shape[1]
    n_blocks = T // Q_BLOCK
    key_pos = jnp.arange(T)
    scale = (QK_NOPE_DIM + QK_ROPE_DIM) ** -0.5
    q = (rmsnorm(c_q, g_q_lat) @ w_uq).reshape(B, T, N_HEADS_B, QK_NOPE_DIM + QK_ROPE_DIM)
    q_nope, q_pe = q[..., :QK_NOPE_DIM], q[..., QK_NOPE_DIM:]
    q_pe = apply_rope(q_pe, cos_b, sin_b)
    kv = (rmsnorm(c_kv, g_kv_lat) @ w_ukv).reshape(B, T, N_HEADS_B, QK_NOPE_DIM + V_DIM_B)
    k_nope, v = kv[..., :QK_NOPE_DIM], kv[..., QK_NOPE_DIM:]
    k_pe = apply_rope(k_rope, cos_b, sin_b)

    def one_block(i):
        s0 = i * Q_BLOCK
        qn = block_slice(q_nope, s0)
        qp = block_slice(q_pe, s0)
        qpos = s0 + jnp.arange(Q_BLOCK)
        causal = key_pos[None, :] <= qpos[:, None]
        s = (jnp.einsum('bqhd,bshd->bhqs', qn, k_nope)
             + jnp.einsum('bqhr,bsr->bhqs', qp, k_pe)).astype(jnp.float32) * scale
        s = jnp.where(causal[None, None], s, -jnp.inf)
        p = jax.nn.softmax(s, axis=-1)
        return jnp.einsum('bhqs,bshd->bqhd', p.astype(v.dtype), v)

    out = lax.map(one_block, jnp.arange(n_blocks))
    return jnp.moveaxis(out, 0, 1).reshape(B, T, N_HEADS_B * V_DIM_B)

def second_inputs(seed: int = 0) -> dict:
    key = jax.random.key(seed)
    ks = jax.random.split(key, 20)

    def w(k, shape, fan_in):
        return jax.random.normal(k, shape, jnp.float32) * (fan_in ** -0.5)

    def gain(k, shape):
        return 1.0 + 0.1 * jax.random.normal(k, shape, jnp.float32)

    L = DEPTH
    return {
        "x": jax.random.normal(ks[0], (BATCH, SEQ, D_MODEL), jnp.float32),
        "g_ffn1": gain(ks[1], (L, D_MODEL)),
        "w1_gate": w(ks[2], (L, D_MODEL, D_FF_2), D_MODEL),
        "w1_up": w(ks[3], (L, D_MODEL, D_FF_2), D_MODEL),
        "w1_down": w(ks[4], (L, D_FF_2, D_MODEL), D_FF_2),
        "g_mix": gain(ks[5], (L, D_MODEL)),
        "w_in": w(ks[6], (L, D_MODEL, D_PROJ), D_MODEL),
        "g_q_lat": gain(ks[7], (L, Q_LORA)),
        "g_kv_lat": gain(ks[8], (L, KV_LORA)),
        "w_uq": w(ks[9], (L, Q_LORA, N_HEADS_B * (QK_NOPE_DIM + QK_ROPE_DIM)), Q_LORA),
        "w_ukv": w(ks[10], (L, KV_LORA, N_HEADS_B * (QK_NOPE_DIM + V_DIM_B)), KV_LORA),
        "w_out": w(ks[11], (L, D_MIX, D_MODEL), D_MIX),
        "g_ffn2": gain(ks[12], (L, D_MODEL)),
        "w2_gate": w(ks[13], (L, D_MODEL, D_FF_2), D_MODEL),
        "w2_up": w(ks[14], (L, D_MODEL, D_FF_2), D_MODEL),
        "w2_down": w(ks[15], (L, D_FF_2, D_MODEL), D_FF_2),
        "g_final": gain(ks[16], (D_MODEL,)),
    }

def second_block(x, g_ffn1, w1_gate, w1_up, w1_down, g_mix, w_in, g_q_lat, g_kv_lat,
              w_uq, w_ukv, w_out, g_ffn2, w2_gate, w2_up, w2_down, g_final):
    B, T, _ = x.shape
    cos_a, sin_a = rope_tables(T, HEAD_DIM_A)
    cos_i, sin_i = rope_tables(T, IDX_DIM)
    cos_b, sin_b = rope_tables(T, QK_ROPE_DIM)
    split_points = [int(v) for v in np.cumsum(PROJ_SIZES)[:-1]]
    for l in range(DEPTH):
        x = x + 0.5 * swiglu(rmsnorm(x, g_ffn1[l]), w1_gate[l], w1_up[l], w1_down[l])
        h = rmsnorm(x, g_mix[l])
        p = h @ w_in[l]
        qa, ka, va, qi, ki, wi, cq, ckv, kr = jnp.split(p, split_points, axis=-1)
        qa = apply_rope(qa.reshape(B, T, N_HEADS_A, HEAD_DIM_A), cos_a, sin_a)
        ka = apply_rope(ka, cos_a, sin_a)
        qi = apply_rope(qi.reshape(B, T, N_IDX_HEADS, IDX_DIM), cos_i, sin_i)
        ki = apply_rope(ki, cos_i, sin_i)
        out_a = dsa_sparse_attention(qa, ka, va, qi, ki, wi)
        out_b = mla_attention(cq, ckv, kr, g_q_lat[l], g_kv_lat[l], w_uq[l], w_ukv[l], cos_b, sin_b)
        x = x + jnp.concatenate([out_a, out_b], axis=-1) @ w_out[l]
        x = x + 0.5 * swiglu(rmsnorm(x, g_ffn2[l]), w2_gate[l], w2_up[l], w2_down[l])
    return rmsnorm(x, g_final)


def setup_inputs(seed=0):
    out = dict(first_inputs(seed))
    for name, value in second_inputs(seed + 1).items():
        if name != "x":
            out[name + "_2"] = value
    return out


def reference(
    x, c, w_ada, b_ada, ln1, ln2, w_in, conv_w, ssm_conv_w, ssm_conv_b, dt_bias, a_log, d_skip,
    ssm_norm_w, w_conv_out, w_ssm_out, w_o, w_up, w_down, final_norm, g_ffn1_2, w1_gate_2,
    w1_up_2, w1_down_2, g_mix_2, w_in_2, g_q_lat_2, g_kv_lat_2, w_uq_2, w_ukv_2, w_out_2,
    g_ffn2_2, w2_gate_2, w2_up_2, w2_down_2, g_final_2,
):
    x = first_block(
        x, c, w_ada, b_ada, ln1, ln2, w_in, conv_w, ssm_conv_w, ssm_conv_b, dt_bias, a_log,
        d_skip, ssm_norm_w, w_conv_out, w_ssm_out, w_o, w_up, w_down, final_norm,
    )
    return second_block(
        x, g_ffn1_2, w1_gate_2, w1_up_2, w1_down_2, g_mix_2, w_in_2, g_q_lat_2, g_kv_lat_2,
        w_uq_2, w_ukv_2, w_out_2, g_ffn2_2, w2_gate_2, w2_up_2, w2_down_2, g_final_2,
    )


_drawn_inputs = setup_inputs


def setup_inputs(seed=0):
    import zlib

    import numpy as np

    out = dict(_drawn_inputs(seed))
    spreads = {}
    factors = {'ssm_conv_b': 8.0,
     'd_skip': 4.972,
     'g_q_lat_2': 5.78,
     'g_kv_lat_2': 3.131,
     'g_ffn2_2': 3.033}
    for name, (base, spread) in spreads.items():
        noise = np.random.default_rng([zlib.crc32(name.encode()), seed]).standard_normal(out[name].shape)
        drawn = base * np.exp(spread * noise) if base else spread * noise
        out[name] = __import__('jax').numpy.asarray(drawn.astype(out[name].dtype))
    for name, factor in factors.items():
        out[name] = (out[name] * factor).astype(out[name].dtype)
    return out
```

```python
from contextlib import ExitStack, contextmanager

import numpy as np

import concourse.bass as bass
from concourse import mybir

F32 = mybir.dt.float32
F32R = mybir.dt.float32r
ALU = mybir.AluOpType
ACT = mybir.ActivationFunctionType
AX_X = mybir.AxisListType.X

P = 128
T = 512
TB = T // P
D = 1024
KB = D // P
UC = 256
UNIT = KB * UC
EPS = 1e-6
NEG = -1e30
TAKEN = -3e38

HEADS, HEAD_DIM = 32, 64
D_SSM = HEADS * HEAD_DIM
GROUPS, STATE = 8, 128
RH = HEADS // GROUPS
GW = RH * HEAD_DIM
CONV_BLOCKS = (D_SSM + 2 * GROUPS * STATE) // P
XB = D_SSM // P
C_GL, C_CB, C_CC, C_CX, C_Z = 0, 2 * D, 3 * D, 4 * D, 5 * D
C_X = C_Z + D_SSM
C_B = C_X + D_SSM
C_C = C_B + GROUPS * STATE
C_DT = C_C + GROUPS * STATE
D_FF = 4 * D
D_FF_2 = 2816
NH, HD = 8, 64
IDX_HEADS = 16
TOPK = 128
ROPE = 32
QH = HD + ROPE
LATB = 5
C_KA, C_QI, C_KI, C_LAT, C_KR = 512, 640, 1664, 1744, 2384
M_VA, M_KI, M_WI, M_KR, M_W = 64, 128, 192, 208, 240
TILES_START = KB
TILES_SCAN = TILES_START + 1 + GROUPS * (6 + 8)
TILES_BEFORE_MIX2 = TILES_SCAN + 8 + 24 + 16 + 8 + 64 + 68
VECS, VROWS = 25, 77
XREADY_END = 8 + 8 + 32 + 8 + 24 + 8 + 24 + 8
FM_ALL = 2 + 8 + 4 + 8 + 8
SOFF = {1: 0, 2: 256, 3: 640}
BOFF = {0: 0, 1: 128, 2: 384, 3: 768}


class Tally:

    def __init__(self, name):
        self.name, self.base, self.per, self.i, self.local = name, 0, 0, None, 0

    def add(self, n=1):
        self.local += n

    def now(self, more=0):
        v = self.base + self.local + more
        return v + self.per * self.i if self.i is not None and self.per else v


class Tallies:

    def __init__(self):
        self.all = {}
        self.per = {}

    def __getattr__(self, name):
        raise AttributeError(name)

    def __getitem__(self, name):
        if name not in self.all:
            self.all[name] = Tally(name)
        return self.all[name]


@contextmanager
def turns(eng, n, tallies, per):
    for name in per:
        tallies[name]
    with eng.Fori(0, n) as i:
        for t in tallies.all.values():
            t.base, t.local, t.i, t.per = t.base + t.local, 0, i, per.get(t.name, 0)
        yield i
    wrong = {t.name: t.local for t in tallies.all.values() if t.local != t.per}
    assert not wrong, f"a turn moves {wrong}"
    for t in tallies.all.values():
        t.base, t.local, t.i, t.per = t.base + t.per * n, 0, None, 0


def r32(ap):
    return ap.bitcast(F32)


def build(nc, a, out):
    ctx = ExitStack()
    with ctx:
        def sem(name):
            return ctx.enter_context(nc.semaphore(name))

        def fixed(name, shape, dt=F32):
            return ctx.enter_context(nc.sbuf_tensor(name, shape, dt))

        raw = [fixed(f"raw{s}", [P, UNIT]) for s in range(2)]
        whi = [fixed(f"whi{s}", [P, UNIT], F32R) for s in range(2)]
        wlo = [fixed(f"wlo{s}", [P, UNIT], F32R) for s in range(2)]
        xT = fixed("xT", [P, KB, T])
        sq = fixed("sq", [P, 2, T])
        ss = fixed("ss", [P, T])
        rinv = fixed("rinv", [P, T])
        ident = fixed("ident", [P, P])
        triu = fixed("triu", [P, P])
        ones = fixed("ones", [P, P])
        v1 = fixed("v1", [P, P])
        v2 = fixed("v2", [P, P])
        v3 = fixed("v3", [P, P])
        v1T = fixed("v1T", [P, 4, CONV_BLOCKS])
        v2T = fixed("v2T", [P, P])
        v3T = fixed("v3T", [P, P])
        cact = fixed("cact", [P, KB])
        modT = fixed("modT", [P, 6, KB])
        coef = fixed("coef", [P, KB])
        epsT = fixed("epsT", [P, 1])
        dskip = fixed("dskip", [XB, 2])
        ln1T, ln2T = v2T[:, 0:8], v2T[:, 8:16]
        badaT, cT = v2T[:, 16:64], v2T[:, 64:72]
        convb0, convw0 = 72, 104
        finalT, gf1T, gmixT, gf2T, gfinT = (v3T[:, 32 + 8 * j:40 + 8 * j] for j in range(5))
        dskip0, normw0, latg0 = 0, 16, 72

        G = [ctx.enter_context(nc.psum_tensor(f"G{b}", [P, T], F32)) for b in range(4)]
        X = [ctx.enter_context(nc.psum_tensor(f"X{b}", [P, T], F32)) for b in range(4)]

        def phase(*specs):
            with ExitStack() as st:
                return [st.enter_context(nc.sbuf_tensor(s[0], s[1], s[2] if len(s) > 2 else F32)) for s in specs]

        split_a = (("ahi", [P, KB, T], F32R), ("alo", [P, KB, T], F32R))

        def after_a(tag, *specs):
            return phase(*((n + tag, s, d) for n, s, d in split_a), *specs)[2:]

        ahi, alo, xin, araw0, araw1, adacc = phase(
            *split_a, ("xin", [P, TB, D]), ("araw0", [P, UNIT]), ("araw1", [P, UNIT]), ("adacc", [P, 2, UC]))
        araw = [araw0, araw1]
        (pacc, pre, cv, xf, zs, xdt, xw, btok, sm, seg, bc, states, yf, yhi, ylo, dts, dtw) = after_a(
            "_s", ("pacc", [P, KB, T]), ("pre", [P, 4, 3 + T]), ("cv", [P, 4, T]), ("xf", [P, 4, T]),
            ("zs", [P, 2, T]), ("xdt", [P, TB, GW]), ("xw", [P, TB, GW]), ("btok", [P, TB, P]),
            ("sm", [P, TB, P]), ("seg", [P, RH, T]), ("bc", [P, RH, T]), ("states", [P, 3, GW]),
            ("yf", [P, 2, T]), ("yhi", [P, 2, T], F32R), ("ylo", [P, 2, T], F32R),
            ("dts", [P, 6, TB, HEADS]), ("dtw", [P, 2, HEADS]))
        ytok = xw
        acT = ss
        DT, AC, EAC, TOEND, EEND, TMP = range(6)
        (_, bhi, blo, qc, braw0, braw1, ccs, pb, badacc) = after_a(
            "_c", ("pacc_c", [P, KB, T]), ("bhi", [P, KB, T], F32R), ("blo", [P, KB, T], F32R),
            ("qc", [P, KB, T]), ("braw0", [P, UNIT]), ("braw1", [P, UNIT]),
            ("ccs", [P, 2, T]), ("pb", [P, 2, 2 + T]), ("badacc", [P, 2, UC]))
        braw = [braw0, braw1]
        (_, _, _, chi, clo) = after_a(
            "_m", ("pacc_m", [P, KB, T]), ("bhi_m", [P, KB, T], F32R), ("blo_m", [P, KB, T], F32R),
            ("chi", [P, KB, T], F32R), ("clo", [P, KB, T], F32R))
        (hhi, hlo, gs) = after_a("_f", ("hhi", [P, KB, T], F32R), ("hlo", [P, KB, T], F32R), ("gs", [P, 2, T]))
        (qF, kF, otok, _, qaF, kaF, kiF, va, wix, krt, kk, score, bias, tab64, tab32, qtok, rtmp, lat, vt, qst,
         pT, biasM, nmask, sm1, m8) = phase(
            ("qF", [QH, NH, T]), ("kF", [QH, NH, T]), ("otok", [P, TB, D]), ("otok_pad", [P, D]), ("qaF", [P, 4, T]), ("kaF", [P, T]),
            ("kiF", [P, T]), ("va", [P, TB, HD]), ("wix", [P, TB, IDX_HEADS]), ("krt", [P, TB, ROPE]),
            ("kk", [P, TB, P]), ("score", [P, 1152]), ("bias", [P, 1280]), ("tab64", [P, 2, TB, HD]),
            ("tab32", [P, 2, TB, ROPE]), ("qtok", [P, TB, 4 * QH]), ("rtmp", [P, T]), ("lat", [P, TB, LATB * P]),
            ("vt", [P, TB, D // 2]), ("qst", [P, 2, T]), ("pT", [P, 2, T]), ("biasM", [P, T]), ("nmask", [P, P]),
            ("sm1", [P, 16]), ("m8", [P, 8]))
        (lhi, llo) = after_a("_l", ("lhi", [P, LATB, T], F32R), ("llo", [P, LATB, T], F32R))
        (xout,) = after_a("_x", ("xout", [P, TB, D]))
        pw = sq

        vec_landed, x_landed, c_landed = sem("vec_landed"), sem("x_landed"), sem("c_landed")
        landed = [sem(f"landed{s}") for s in range(2)]
        ada_landed = [sem(f"ada_landed{s}") for s in range(2)]
        tab_landed = sem("tab_landed")
        hi_split, lo_split = sem("hi_split"), sem("lo_split")
        tile_done = sem("tile_done")
        g_free = [sem(f"g_free{b}") for b in range(4)]
        aux_done = sem("aux_done")
        x_free = [sem(f"x_free{b}") for b in range(4)]
        gone = sem("gone")
        dve_step, act_step = sem("dve_step"), sem("act_step")
        vec_ready, mod_ready = sem("vec_ready"), sem("mod_ready")
        x_ready = sem("x_ready")
        sq_ready, ss_added, rt_ready = sem("sq_ready"), sem("ss_added"), sem("rt_ready")
        rinv_ready = sem("rinv_ready")
        val_ready, val_hi = sem("val_ready"), sem("val_hi")
        mask_ready = sem("mask_ready")
        act_ready = sem("act_ready")
        ada_acc, ada_used = sem("ada_acc"), sem("ada_used")
        dskip_ready = sem("dskip_ready")
        sg_ready, sg_used = sem("sg_ready"), sem("sg_used")
        c_ready = sem("c_ready")
        prep_a, prep_v = sem("prep_a"), sem("prep_v")
        acT_ready, pacc_zero = sem("acT_ready"), sem("pacc_zero")
        pre_ready, cv_ready, xf_ready = sem("pre_ready"), sem("cv_ready"), sem("xf_ready")
        xw_ready = sem("xw_ready")
        seg_ready, exp_ready, m_ready = sem("seg_ready"), sem("exp_ready"), sem("m_ready")
        st_ready, ytok_ready, yf_ready = sem("st_ready"), sem("ytok_ready"), sem("yf_ready")
        act_saved, bc_landed = sem("act_saved"), sem("bc_landed")
        k_ready, fm_ready = sem("k_ready"), sem("fm_ready")
        rl_ready, rl_used = sem("rl_ready"), sem("rl_used")
        lat_ready, lat_sum, lat_done = sem("lat_ready"), sem("lat_sum"), sem("lat_done")
        q_staged = [sem(f"q_staged{s}") for s in range(2)]
        lg_ready, p_ready, pT_ready, o_ready = sem("lg_ready"), sem("p_ready"), sem("pT_ready"), sem("o_ready")
        p_used = sem("p_used")
        o_copied, out_done = sem("o_copied"), sem("out_done")

        acum_dram = nc.dram_tensor("acum_dram", [HEADS, T], F32, kind="Internal").ap()

        def cols(w):
            return w.rearrange("(k p) n -> p k n", p=P)

        w_in, w_conv, w_o = cols(a["w_in"][0]), cols(a["w_conv_out"][0]), cols(a["w_o"][0])
        w_ssm = a["w_ssm_out"][0].rearrange("(g b p) n -> p g b n", p=P, b=2)
        w_up, w_down = cols(a["w_up"][0]), cols(a["w_down"][0])
        w_ada = cols(a["w_ada"][0])
        ffn = [[cols(a[f"w{j}_{n}_2"][0]) for n in ("gate", "up", "down")] for j in (1, 2)]
        w_in2, w_uq, w_ukv, w_out = (cols(a[n][0]) for n in ("w_in_2", "w_uq_2", "w_ukv_2", "w_out_2"))

        def unit(t, k=KB, n=UC):
            return t[:, 0:k * n].rearrange("p (k n) -> p k n", k=k)

        block = ctx.enter_context(nc.Block())

        @block.sync
        def _(sp):
            t = Tallies()
            slot = [0]
            started = [0]

            def load(*pieces, k=KB, n=UC):
                s = slot[0]
                slot[0] ^= 1
                if started[0] >= 2:
                    sp.wait_ge(lo_split, t["n"].now(-1))
                started[0] += 1
                at = 0
                for src in pieces:
                    w = src.shape[-1]
                    dst = unit(raw[s], k, n)[:, :, at:at + w]
                    sp.dma_start(dst, src).then_inc(landed[s], 16)
                    at += w
                t["n"].add()

            def load_ada(buf, dst, unit_no, first):
                if not first:
                    sp.wait_ge(ada_acc, t["ada"].now(-1))
                sp.dma_start(unit(dst), w_ada[:, :, bass.ds(unit_no * UC, UC)]).then_inc(ada_landed[buf], 16)
                t["ada"].add()

            def vec(dst, src):
                sp.dma_start(dst, src).then_inc(vec_landed, 16)

            def rows(v):
                return v.rearrange("(b p) -> b p", p=P)

            vec(v2[0:8, :], rows(a["ln1"][0]))
            vec(v2[8:16, :], rows(a["ln2"][0]))
            vec(v2[16:64, :], rows(a["b_ada"][0]))
            vec(v2[64:72, :], rows(a["c"][0]))
            vec(v2[72:104, :], rows(a["ssm_conv_b"][0]))
            for j in range(3):
                vec(v2[104 + 8 * j:112 + 8 * j, :], rows(a["conv_w"][0, j]))
            for j in range(4):
                vec(v1[32 * j:32 * j + 32, :], rows(a["ssm_conv_w"][0, j]))
            vec(ident[:], a["ident"])
            for b in range(2):
                load_ada(b, araw[b], b, True)
            at = XB
            for name, n in (("ssm_norm_w", 16), ("final_norm", 8), ("g_ffn1_2", 8), ("g_mix_2", 8),
                            ("g_ffn2_2", 8), ("g_final_2", 8), ("g_q_lat_2", 3), ("g_kv_lat_2", 2)):
                v = a[name] if len(a[name].shape) == 1 else a[name][0]
                vec(v3[at:at + n, :], rows(v))
                at += n
            vec(dskip[:], a["d_skip"][0].rearrange("(b r) -> b r", r=2))
            vec(triu[:], a["triu"])
            vec(dtw[:, 0, :], a["dt_bias"].broadcast_to([P, HEADS]))
            vec(dtw[:, 1, :], a["a_log"].broadcast_to([P, HEADS]))
            for b in range(2, 8):
                load_ada(b % 2, araw[b % 2], b, False)

            def bc_load(g):
                if t["seg"].now() is not 0:
                    sp.wait_ge(seg_ready, t["seg"].now())
                src = acum_dram[bass.ds(g * RH, RH), :].rearrange("r t -> (r t)").unsqueeze(0)
                sp.dma_start(bc[:].rearrange("p r t -> p (r t)"), src.broadcast_to([P, RH * T])).then_inc(bc_landed, 16)

            def scan_turn(g, gemm, ssd, outp):
                if gemm:
                    load(w_in[:, :, bass.ds(C_X + g * GW, GW)])
                if g is 1:
                    sp.wait_ge(acT_ready, 1)
                    sp.dma_start(acum_dram, acT[0:HEADS, :]).then_inc(act_saved, 16)
                    sp.wait_ge(act_saved, 16)
                if outp:
                    sl = slot[0]
                    slot[0] ^= 1
                    sp.wait_ge(lo_split, t["n"].now(-1))
                    sp.dma_start(raw[sl][:, :].rearrange("p (o b n) -> p o b n", o=1, b=2),
                                 w_ssm[:, bass.ds(g - 2, 1), :, :]).then_inc(landed[sl], 16)
                    t["n"].add()
                if ssd:
                    bc_load(g - 1)
                    t["seg"].add(RH)
                if gemm:
                    load(w_in[:, :, bass.ds(C_B + g * STATE, STATE)], w_in[:, :, bass.ds(C_C + g * STATE, STATE)])
                    load(w_in[:, :, bass.ds(C_Z + g * GW, GW)])

            load(w_in[:, :, C_DT:C_DT + HEADS], n=HEADS)
            scan_turn(0, True, False, False)
            scan_turn(1, True, True, False)
            with turns(sp, GROUPS - 2, t, {"n": 4, "seg": RH}) as i:
                scan_turn(i + 2, True, True, True)
            scan_turn(GROUPS, False, True, True)
            scan_turn(GROUPS + 1, False, False, True)

            with turns(sp, 2, t, {"n": 2, "ada": 2}) as i:
                for m in range(2):
                    load(w_in[:, :, bass.ds(C_GL + D + (2 * i + m) * UC, UC)])
                sp.wait_ge(tile_done, TILES_SCAN)
                for m in range(2):
                    load_ada(m, braw[m], 8 + 2 * i + m, False)
            with turns(sp, 4, t, {"n": 2, "ada": 2}) as i:
                load(w_in[:, :, bass.ds(C_CC + i * UC, UC)])
                load(w_in[:, :, bass.ds(C_CX + i * UC, UC)])
                for m in range(2):
                    load_ada(m, braw[m], 12 + 2 * i + m, False)
            with turns(sp, 2, t, {"n": 2, "ada": 2}) as i:
                for m in range(2):
                    load(w_in[:, :, bass.ds(C_CB + (2 * i + m) * UC, UC)])
                for m in range(2):
                    load_ada(m, braw[m], 20 + 2 * i + m, False)
            with turns(sp, 4, t, {"n": 2}) as i:
                load(w_in[:, :, bass.ds(C_GL + i * UC, UC)])
                load(w_conv[:, :, bass.ds(i * UC, UC)])
            with turns(sp, 2, t, {"n": 2}) as i:
                for m in range(2):
                    load(w_o[:, :, bass.ds((2 * i + m) * UC, UC)])
            with turns(sp, 4, t, {"n": 8}) as i:
                for j in range(4):
                    load(w_up[:, :, bass.ds(i * D + j * UC, UC)])
                for j in range(4):
                    load(w_down[:, bass.ds(i * KB, KB), j * UC:(j + 1) * UC])

            def swiglu(w):
                gate, up, down = w
                with turns(sp, 2, t, {"n": 12}) as i:
                    for j in range(4):
                        load(gate[:, :, bass.ds(i * D + j * UC, UC)])
                        load(up[:, :, bass.ds(i * D + j * UC, UC)])
                    for j in range(4):
                        load(down[:, bass.ds(i * KB, KB), j * UC:(j + 1) * UC])
                for j in range(3):
                    load(gate[:, :, 2 * D + j * UC:2 * D + (j + 1) * UC])
                    load(up[:, :, 2 * D + j * UC:2 * D + (j + 1) * UC])
                for j in range(4):
                    load(down[:, 16:22, j * UC:(j + 1) * UC], k=6)

            swiglu(ffn[0])
            load(w_in2[:, :, C_KA:C_QI], w_in2[:, :, C_KI:C_LAT], w_in2[:, :, C_KR:C_KR + ROPE])
            sp.wait_ge(tile_done, TILES_BEFORE_MIX2)
            sp.dma_start(tab64[:, 0], a["cos64"].rearrange("(b p) n -> p b n", p=P)).then_inc(tab_landed, 16)
            sp.dma_start(tab64[:, 1], a["sin64"].rearrange("(b p) n -> p b n", p=P)).then_inc(tab_landed, 16)
            sp.dma_start(tab32[:, 0], a["cos32"].rearrange("(b p) n -> p b n", p=P)).then_inc(tab_landed, 16)
            sp.dma_start(tab32[:, 1], a["sin32"].rearrange("(b p) n -> p b n", p=P)).then_inc(tab_landed, 16)
            sp.dma_start(nmask[:], a["nmask"]).then_inc(tab_landed, 16)
            for j in range(4):
                load(w_in2[:, :, C_QI + j * UC:C_QI + (j + 1) * UC])
            for j in range(2):
                load(w_in2[:, :, j * UC:(j + 1) * UC])
            for j in range(3):
                w = min(UC, C_KR - C_LAT - j * UC)
                load(w_in2[:, :, C_LAT + j * UC:C_LAT + j * UC + w])
            for j in range(2):
                load(w_uq[:, :, j * 4 * QH:(j + 1) * 4 * QH], k=3, n=4 * QH)
            for j in range(2):
                load(w_ukv[:, :, j * T:(j + 1) * T], k=2, n=T)
            for j in range(2):
                load(w_out[:, :, j * UC:(j + 1) * UC])
            sp.wait_ge(fm_ready, FM_ALL)
            sp.dma_start(qst[:, 0, :].unsqueeze(1), qaF[:, 0:1, :]).then_inc(q_staged[0], 16)
            with turns(sp, NH // 2 - 1, t, {"q": 2 * TB}) as i:
                t["q"].add(2 * TB)
                sp.wait_ge(lg_ready, t["q"].now())
                sp.dma_start(qst[:, 0, :].unsqueeze(1), qaF[:, bass.ds(i + 1, 1), :]).then_inc(q_staged[0], 16)
            t["q"].add(2 * TB)
            sp.wait_ge(lg_ready, t["q"].now())
            with turns(sp, NH // 2, t, {"q": 2 * TB}) as i:
                for s in range(2):
                    sp.wait_ge(lg_ready, t["q"].now(TB * (s - 1)))
                    sp.dma_start(qst[0:QH, s, :].unsqueeze(1), qF[:, bass.ds(2 * i + s, 1), :])\
                        .then_inc(q_staged[s], 16)
                t["q"].add(2 * TB)
            for j in range(2, 4):
                load(w_out[:, :, j * UC:(j + 1) * UC])
            swiglu(ffn[1])
            for b in range(TB):
                sp.wait_ge(o_copied, 2 * (b + 1))
                sp.dma_start(out[0, b * P:(b + 1) * P, :], xout[:, b, :]).then_inc(out_done, 16)
            sp.wait_ge(out_done, 16 * TB)

        @block.tensor
        def _(pe):
            t = Tallies()
            slot = [0]

            def next_unit():
                s = slot[0]
                slot[0] ^= 1
                t["n"].add()
                pe.wait_ge(lo_split, t["n"].now())
                return s

            def take_g(b):
                used = t[f"g{b}"]
                if used.i is not None or used.now() != 0:
                    pe.wait_ge(g_free[b], used.now())
                used.add()
                return G[b]

            def take_x(b):
                used = t[f"x{b}"]
                if used.i is not None or used.now() != 0:
                    pe.wait_ge(x_free[b], used.now())
                used.add()
                return X[b]

            def fm_tile(s, m, rh, rl, k=KB, n=UC, b=None, each=None):
                bank = take_g(2 * s + m if b is None else b)
                wh, wl = unit(whi[s], k, n), unit(wlo[s], k, n)
                f = slice(m * P, (m + 1) * P)
                for j in range(k):
                    if each is not None:
                        pe.wait_ge(act_ready, each.now(j + 1))
                    pe.matmul(bank[:], wh[:, j, f], rh[:, j, :], start=(j == 0), stop=False)
                    pe.matmul(bank[:], wh[:, j, f], rl[:, j, :], start=False, stop=False)
                    last = pe.matmul(bank[:], wl[:, j, f], rh[:, j, :], start=False, stop=(j == k - 1))
                last.then_inc(tile_done, 1)

            def fm_unit(rh, rl, k=KB, each=None):
                s = next_unit()
                for m in range(2):
                    fm_tile(s, m, rh, rl, k, each=each if m == 0 else None)

            def tok_part(dst, s, b, k, n, rh, rl, width=None):
                wh, wl = unit(whi[s], k, width or n), unit(wlo[s], k, width or n)
                tk = slice(b * P, (b + 1) * P)
                for j in range(k):
                    pe.matmul(dst, rh[:, j, tk], wh[:, j, 0:n], start=(j == 0), stop=False)
                    pe.matmul(dst, rl[:, j, tk], wh[:, j, 0:n], start=False, stop=False)
                    last = pe.matmul(dst, rh[:, j, tk], wl[:, j, 0:n], start=False, stop=(j == k - 1))
                return last

            def tok_unit(n=UC):
                s = next_unit()
                for half in range(2):
                    bank = take_g(2 * s + half)
                    for b in range(2):
                        last = tok_part(bank[:, b * UC:b * UC + n], s, 2 * half + b, KB, n, ahi, alo, UC)
                    last.then_inc(tile_done, 1)

            def column_sum():
                t["ss"].add(KB - 1)
                bank = take_x(1)
                pe.wait_ge(ss_added, t["ss"].now())
                pe.matmul(bank[:], ones[:], ss[:], start=True, stop=True).then_inc(aux_done, 1)

            def operand(n):
                t["op"].add(n)
                pe.wait_ge(act_ready, t["op"].now())

            pe.wait_ge(dskip_ready, 1)
            pe.wait_ge(vec_landed, 16 * VECS)
            bank = take_x(0)
            pe.transpose(bank[:, 0:P], v1[:], ident[:])
            pe.transpose(bank[:, P:2 * P], v2[:], ident[:])
            pe.transpose(bank[:, 2 * P:2 * P + VROWS], v3[0:VROWS, :], ident[0:VROWS, 0:VROWS]).then_inc(aux_done, 1)
            pe.wait_ge(x_landed, 16)
            for k in range(KB):
                bank = take_g(k % 4)
                for b in range(TB):
                    last = pe.transpose(bank[:, b * P:(b + 1) * P], xin[:, b, k * P:(k + 1) * P], ident[:])
                last.then_inc(tile_done, 1)

            acc = [adacc]

            def ada_columns(at):
                b = t["ada"].local % 2
                t["ada"].add()
                pe.wait_ge(ada_acc, t["ada"].now())
                for m in range(2):
                    last = pe.matmul(X[3][:, bass.ds(at + m, 1)], acc[0][:, b, m * P:(m + 1) * P],
                                     ones[:, 0:1], start=True, stop=True)
                last.then_inc(ada_used, 1)

            pe.wait_ge(gone, 1)
            column_sum()
            take_x(3)
            for u in range(8):
                ada_columns(2 * u)

            operand(KB)
            s = next_unit()
            bank = take_g(2 * s)
            for b in range(TB):
                last = tok_part(bank[:, b * HEADS:(b + 1) * HEADS], s, b, KB, HEADS, ahi, alo)
            last.then_inc(tile_done, 1)

            def scan_turn(gemm, ssd, outp):
                if gemm:
                    sx = next_unit()
                    fm_tile(sx, 0, ahi, alo)
                if outp:
                    t["ss"].add(1)
                    bank = take_x(2)
                    pe.wait_ge(ss_added, t["ss"].now())
                    pe.matmul(bank[:], ones[:], ss[:], start=True, stop=True).then_inc(aux_done, 1)
                if gemm:
                    fm_tile(sx, 1, ahi, alo)
                if outp:
                    s = next_unit()
                    operand(2)
                    for m in range(KB):
                        fm_tile(s, m, yhi, ylo, k=2, n=D, b=2 * s + m % 2)
                if ssd:
                    t["xf"].add(4)
                    pe.wait_ge(xf_ready, t["xf"].now())
                    for half in range(2):
                        bank = take_x(half)
                        for c in range(2):
                            ck = slice((2 * half + c) * P, (2 * half + c + 1) * P)
                            for b in range(2):
                                last = pe.transpose(bank[:, c * GW + b * P:c * GW + (b + 1) * P], xf[:, b, ck], ident[:])
                        last.then_inc(aux_done, 1)
                    bank = take_x(2)
                    for c in range(TB):
                        last = pe.transpose(bank[:, c * P:(c + 1) * P], xf[:, 2, c * P:(c + 1) * P], ident[:])
                    last.then_inc(aux_done, 1)
                    bank = take_x(3)
                    for c in range(TB):
                        ck = slice(c * P, (c + 1) * P)
                        last = pe.matmul(bank[:, ck], xf[:, 2, ck], xf[:, 3, ck], start=True, stop=True)
                    last.then_inc(aux_done, 1)
                if gemm:
                    fm_unit(ahi, alo)
                if ssd:
                    y0, y1 = take_x(0), take_x(1)
                    for r in range(RH):
                        t["m"].add()
                        pe.wait_ge(m_ready, t["m"].now())
                        for c in range(TB):
                            bank = (y0, y1)[c // 2]
                            at = (c % 2) * GW + r * HEAD_DIM
                            last = pe.matmul(bank[:, at:at + HEAD_DIM], seg[:, r, c * P:(c + 1) * P],
                                             xdt[:, c, r * HEAD_DIM:(r + 1) * HEAD_DIM], start=True, stop=True)
                    last.then_inc(aux_done, 1)
                    bank, bank3 = take_x(2), take_x(3)
                    t["xw"].add()
                    pe.wait_ge(xw_ready, t["xw"].now())
                    for c in range(3):
                        dst = bank3[:, 0:GW] if c == 2 else bank[:, c * GW:(c + 1) * GW]
                        last = pe.matmul(dst, btok[:, c, :], xw[:, c, :], start=True, stop=True)
                    last.then_inc(aux_done, 1)
                if gemm:
                    sz = next_unit()
                    fm_tile(sz, 0, ahi, alo)
                if ssd:
                    bank, bank3 = take_x(2), take_x(3)
                    t["st"].add()
                    pe.wait_ge(st_ready, t["st"].now())
                    for c in range(1, TB):
                        dst = bank3[:, 0:GW] if c == 3 else bank[:, (c - 1) * GW:c * GW]
                        last = pe.matmul(dst, xf[:, 3, c * P:(c + 1) * P], states[:, c - 1, :], start=True, stop=True)
                    last.then_inc(aux_done, 1)
                if gemm:
                    fm_tile(sz, 1, ahi, alo)
                if ssd:
                    t["yt"].add()
                    pe.wait_ge(ytok_ready, t["yt"].now())
                    for b in range(2):
                        bank = take_x(b)
                        for c in range(TB):
                            last = pe.transpose(bank[:, c * P:(c + 1) * P], ytok[:, c, b * P:(b + 1) * P], ident[:])
                        last.then_inc(aux_done, 1)

            scan_turn(True, False, False)
            bank, bank1, bank2 = take_x(0), take_x(1), take_x(2)
            pe.wait_ge(prep_v, 3)
            decays = dts[:, TMP, :, :]
            pe.matmul(bank[:, 0:P], triu[:], decays, start=True, stop=True).then_inc(aux_done, 1)
            pe.matmul(bank1[:, 0:P], ones[:], decays, start=True, stop=True).then_inc(aux_done, 1)
            for c in range(TB):
                last = pe.matmul(bank2[0:HEADS, c * P:(c + 1) * P], dts[:, TMP, c, :], triu[:], start=True, stop=True)
            last.then_inc(aux_done, 1)
            scan_turn(True, True, False)
            with turns(pe, GROUPS - 2, t, {"n": 4, "g0": 5, "g1": 5, "g2": 2, "g3": 2, "x0": 3, "x1": 3, "x2": 4,
                                           "x3": 3, "ss": 1, "op": 2, "xf": 4, "m": 4, "xw": 1, "st": 1, "yt": 1}
                       ):
                scan_turn(True, True, True)
            scan_turn(False, True, True)
            scan_turn(False, False, True)

            acc[0] = badacc
            take_x(3)
            both = {"n": 2, "g0": 1, "g1": 1, "g2": 1, "g3": 1}
            with turns(pe, 2, t, {**both, "ada": 2}) as i:
                for m in range(2):
                    fm_unit(ahi, alo)
                for m in range(2):
                    ada_columns(16 + 4 * i + 2 * m)
            with turns(pe, 4, t, {**both, "ada": 2}) as i:
                for m in range(2):
                    fm_unit(ahi, alo)
                for m in range(2):
                    ada_columns(24 + 4 * i + 2 * m)
            with turns(pe, 2, t, {**both, "ada": 2}) as i:
                for m in range(2):
                    fm_unit(ahi, alo)
                for m in range(2):
                    ada_columns(40 + 4 * i + 2 * m)
            operand(KB)
            with turns(pe, 4, t, both):
                fm_unit(ahi, alo)
                fm_unit(bhi, blo)
            operand(KB)
            with turns(pe, 2, t, both):
                for m in range(2):
                    fm_unit(chi, clo)

            def slab(ups, k, per=None):
                for j in range(ups):
                    fm_unit(ahi, alo)
                for j in range(4):
                    fm_unit(hhi, hlo, k, each=t["op"] if j == 0 else None)
                t["op"].add(k)

            column_sum()
            operand(KB)
            with turns(pe, 4, t, {"n": 8, "g0": 4, "g1": 4, "g2": 4, "g3": 4, "op": KB}):
                slab(4, KB)

            def swiglu():
                column_sum()
                operand(KB)
                with turns(pe, 2, t, {"n": 12, "g0": 6, "g1": 6, "g2": 6, "g3": 6, "op": KB}):
                    slab(8, KB)
                slab(6, 6)

            column_sum()
            swiglu()

            column_sum()
            operand(KB)
            tok_unit(M_W)
            t["k"].add(2)
            pe.wait_ge(k_ready, t["k"].now())
            kview = qtok[:, :, 0:P]
            for b2, src in ((0, kk), (1, kview)):
                bank = take_x(b2)
                for b in range(TB):
                    last = pe.transpose(bank[:, b * P:(b + 1) * P], src[:, b, :], ident[:])
                last.then_inc(aux_done, 1)

            def turn_heads(pairs=True):
                t["k"].add()
                pe.wait_ge(k_ready, t["k"].now())
                for j in range(2 if pairs else 4):
                    bank = take_x(j % 2)
                    w = P if pairs else QH
                    for b in range(TB):
                        last = pe.transpose(bank[0:w, b * P:(b + 1) * P], qtok[:, b, j * w:(j + 1) * w], ident[:])
                    last.then_inc(aux_done, 1)

            def index_scores():
                t["fm"].add(2)
                pe.wait_ge(fm_ready, t["fm"].now())
                for j in range(2):
                    for h in range(2):
                        rows = slice(h * HD, (h + 1) * HD)
                        for q in range(1, TB):
                            bank = take_x(2 + t["rot"].local % 2)
                            t["rot"].add()
                            w = (q + 1) * P
                            pe.matmul(bank[:, 0:w], qst[rows, j, q * P:(q + 1) * P], kiF[rows, 0:w],
                                      start=True, stop=True).then_inc(aux_done, 1)

            t["fm"].add(2)
            for u in range(4):
                tok_unit()
                if u:
                    index_scores()
                turn_heads()
            for u in range(2):
                tok_unit()
                if u == 0:
                    index_scores()
                turn_heads()
            for u in range(3):
                tok_unit(min(UC, LATB * P - u * UC))
            pe.wait_ge(lat_done, 1)
            for j in range(LATB):
                bank = take_x(j % 2)
                for b in range(TB):
                    last = pe.transpose(bank[:, b * P:(b + 1) * P], lat[:, b, j * P:(j + 1) * P], ident[:])
                last.then_inc(aux_done, 1)
            operand(LATB)

            def latent_unit(first, k, n):
                s = next_unit()
                for b in range(TB):
                    bank = take_g(2 * s + b % 2)
                    tok_part(bank[:, 0:n], s, b, k, n, lhi[:, first:first + k, :], llo[:, first:first + k, :])\
                        .then_inc(tile_done, 1)

            for u in range(2):
                latent_unit(0, 3, 4 * QH)
                turn_heads(False)
            for u in range(2):
                latent_unit(3, 2, T)
                turn_heads(False)

            t["rot"].base, t["rot"].local = 0, 0
            for latent in range(2):
                with turns(pe, NH // 2, t, {"qs0": 16, "qs1": 16 * latent, "x0": 4, "x1": 4, "x2": 8, "x3": 8, "p": 8}) as i:
                    items = [(h, q) for h in range(2) for q in range(TB)]

                    def logits(n):
                        h, q = items[n]
                        if q == 0 and (latent or h == 0):
                            t[f"qs{h}"].add(16)
                            pe.wait_ge(q_staged[h], t[f"qs{h}"].now())
                        w = (q + 1) * P
                        bank = take_x(n % 2)
                        if latent:
                            lhs, rhs = qst[0:QH, h, q * P:(q + 1) * P], kF[:, bass.ds(2 * i + h, 1), 0:w]
                        else:
                            rows = slice(h * HD, (h + 1) * HD)
                            lhs, rhs = qst[rows, 0, q * P:(q + 1) * P], kaF[rows, 0:w]
                        pe.matmul(bank[:, 0:w], lhs, rhs, start=True, stop=True).then_inc(aux_done, 1)
                        
                    def turn_p(n):
                        h, q = items[n]
                        t["p"].add()
                        bank = take_x(2)
                        pe.wait_ge(p_ready, t["p"].now())
                        for j in range(q + 1):
                            last = pe.transpose(bank[:, j * P:(j + 1) * P], pw[:, n % 2, j * P:(j + 1) * P], ident[:])
                        last.then_inc(aux_done, 1)

                    def values(n):
                        h, q = items[n]
                        bank = take_x(3)
                        pe.wait_ge(pT_ready, t["p"].now(0 if n == len(items) - 1 else -1))
                        for j in range(q + 1):
                            v = vt[:, j, bass.ds((2 * i + h) * HD, HD)] if latent else va[:, j, :]
                            last = pe.matmul(bank[:, 0:HD], pT[:, n % 2, j * P:(j + 1) * P], v,
                                             start=(j == 0), stop=(j == q))
                        last.then_inc(aux_done, 1)

                    for n in range(len(items) + 2):
                        if n < len(items):
                            logits(n)
                        if 1 <= n <= len(items):
                            turn_p(n - 1)
                        if n >= 2:
                            values(n - 2)
            pe.wait_ge(o_ready, 1)
            for k in range(KB):
                bank = take_x(k % 4)
                for b in range(TB):
                    last = pe.transpose(bank[:, b * P:(b + 1) * P], otok[:, b, k * P:(k + 1) * P], ident[:])
                last.then_inc(aux_done, 1)
            operand(KB)
            for u in range(4):
                fm_unit(ahi, alo)
            swiglu()
            column_sum()
            pe.wait_ge(x_ready, XREADY_END)
            for b in range(TB):
                for half in range(2):
                    bank = take_x(2 * (b % 2) + half)
                    for j in range(4):
                        last = pe.transpose(bank[:, j * P:(j + 1) * P], xT[:, 4 * half + j, b * P:(b + 1) * P], ident[:])
                    last.then_inc(aux_done, 1)

        @block.scalar
        def _(act):
            t = Tallies()
            slot = [0]

            def split_next(loads=1):
                s = slot[0]
                slot[0] ^= 1
                t[f"land{s}"].add(16 * loads)
                act.wait_ge(landed[s], t[f"land{s}"].now())
                if s or t["tile"].i is not None or t["tile"].now():
                    act.wait_ge(tile_done, t["tile"].now())
                act.activation(whi[s][:], raw[s][:], ACT.Copy).then_inc(hi_split, 1)

            def tile():
                t["tile"].add()
                act.wait_ge(tile_done, t["tile"].now())

            def aux():
                t["aux"].add()
                act.wait_ge(aux_done, t["aux"].now())

            def link(ins):
                t["step"].add()
                ins.then_inc(act_step, 1)
                act.wait_ge(act_step, t["step"].now())

            def squares():
                for k in range(KB):
                    t["x"].add()
                    act.wait_ge(x_ready, t["x"].now())
                    if k >= 2:
                        act.wait_ge(ss_added, t["ss"].now(max(1, k - 2)))
                    act.activation(sq[:, k % 2, :], xT[:, k, :], ACT.Square).then_inc(sq_ready, 1)
                t["ss"].add(KB - 1)

            def root(bank, b, width):
                aux()
                act.activation(rinv[:], bank[:], ACT.Sqrt, bias=epsT[:], scale=1.0 / width).then_inc(rt_ready, 1)

            def high(dst, src, bias=None):
                t["val"].add()
                act.wait_ge(val_ready, t["val"].now())
                if bias is None:
                    act.activation(dst, src, ACT.Copy).then_inc(val_hi, 1)
                else:
                    act.activation(dst, src, ACT.Identity, bias=bias).then_inc(val_hi, 1)

            def norm(hi=None, lo_bias=None):
                squares()
                root(X[1], 1, D)
                if hi is not None:
                    for k in range(KB):
                        high(hi[:, k, :], sq[:, k % 2, :], None if lo_bias is None else lo_bias[:, k:k + 1])

            act.dma_start(xin[:], a["x"][0].rearrange("(b p) n -> p b n", p=P)).then_inc(x_landed, 16)
            act.wait_ge(vec_ready, 1)
            act.activation(cact[:], cT, ACT.Silu).then_inc(c_ready, 1)
            act.wait_ge(gone, 2)
            t["aux"].add()
            t["tile"].add(KB)
            squares()
            root(X[1], 1, D)
            t["land0"].add(16)
            act.wait_ge(landed[0], 16)
            slot[0] = 1
            act.activation(whi[0][:, 0:KB * HEADS], raw[0][:, 0:KB * HEADS], ACT.Copy).then_inc(hi_split, 1)
            for k in range(KB):
                high(ahi[:, k, :], sq[:, k % 2, :], modT[:, 0, k:k + 1])

            split_next()
            t["tile"].add()
            act.wait_ge(prep_v, 1)
            z, e, w = dts[:, TMP], dts[:, DT], dts[:, AC]
            link(act.activation(e, z, ACT.Abs))
            link(act.activation(e, e, ACT.Exp, scale=-1.0))
            act.activation(dtw[:, 1, :], dtw[:, 1, :], ACT.Exp).then_inc(prep_a, 1)
            act.wait_ge(prep_v, 2)
            act.activation(dts[:, EAC], w, ACT.Ln).then_inc(prep_a, 1)

            def unit(loads=1):
                s = slot[0] ^ 1
                split_next(loads)
                return s

            def conv_in(b, m, blk):
                tile()
                act.activation(cv[:, m, :], G[b][:], ACT.Identity, scale=v1T[:, 3, bass.ds(blk, 1)],
                               bias=v2T[:, bass.ds(convb0 + blk, 1)])
                act.activation(pre[:, m, 3:3 + T], G[b][:], ACT.Copy).then_inc(pre_ready, 1)

            def scan_turn(g, gemm, ssd, outp):
                if gemm:
                    s = unit(1 if outp else 2)
                    if t["xf"].i is not None or t["xf"].now():
                        act.wait_ge(xf_ready, t["xf"].now())
                    conv_in(2 * s, 0, 2 * g)
                if outp:
                    root(X[2], 2, GW)
                if gemm:
                    conv_in(2 * s + 1, 1, 2 * g + 1)
                if outp:
                    for b in range(2):
                        high(yhi[:, b, :], sq[:, b, :])
                    unit(2 if gemm else 1)
                    t["tile"].add(KB)
                if gemm:
                    s = unit()
                if ssd:
                    t["aux"].add(2)
                    aux()
                    act.activation(btok[:], X[2][:].rearrange("p (c n) -> p c n", c=TB), ACT.Copy)\
                        .then_inc(x_free[2], 1)
                    t["aux"].add(1)
                    for r in range(RH):
                        t["seg"].add()
                        act.wait_ge(seg_ready, t["seg"].now())
                        act.activation(seg[:, r, :], seg[:, r, :], ACT.Exp).then_inc(exp_ready, 1)
                if gemm:
                    for m in range(2):
                        conv_in(2 * s + m, 2 + m, XB + GROUPS * m + g)
                    s = unit()
                if ssd:
                    t["aux"].add(1 + 1 + 1 + 2)
                    for b in range(2):
                        t["yf"].add()
                        act.wait_ge(yf_ready, t["yf"].now())
                        act.activation(sq[:, b, :], yf[:, b, :], ACT.Square).then_inc(sq_ready, 1)
                if gemm:
                    for m in range(2):
                        tile()
                        act.activation(zs[:, m, :], G[2 * s + m][:], ACT.Silu).then_inc(g_free[2 * s + m], 1)
                    for b in range(4):
                        t["cv"].add()
                        act.wait_ge(cv_ready, t["cv"].now())
                        act.activation(xf[:, b, :], cv[:, b, :], ACT.Silu).then_inc(xf_ready, 1)
                    t["xf"].add(4)

            scan_turn(0, True, False, False)
            t["aux"].add(2)
            aux()
            act.activation(acT[0:HEADS, :], X[2][0:HEADS, :], ACT.Copy).then_inc(acT_ready, 1)
            act.wait_ge(prep_v, 4)
            act.activation(dts[:, EAC], X[0][:, 0:P].rearrange("p (c h) -> p c h", c=TB), ACT.Exp)
            act.activation(dts[:, EEND], X[1][:, 0:P].rearrange("p (c h) -> p c h", c=TB), ACT.Exp)
            act.activation(dts[:, TOEND], dts[:, TOEND], ACT.Exp).then_inc(prep_a, 1)
            scan_turn(1, True, True, False)
            with turns(act, GROUPS - 2, t, {"land0": 32, "land1": 48, "tile": 14, "aux": 10, "ss": 0, "val": 2,
                                            "xf": 4, "seg": 4, "yf": 2, "cv": 4}) as i:
                scan_turn(i + 2, True, True, True)
            scan_turn(GROUPS, False, True, True)
            scan_turn(GROUPS + 1, False, False, True)
            t["ss"].add(GROUPS)

            def gated(dst, s, m, func, used=False):
                tile()
                if used and m == 0:
                    act.wait_ge(sg_used, t["sg"].now())
                if used:
                    t["sg"].add()
                act.activation(dst, G[2 * s + m][:], func).then_inc(sg_ready, 1)

            both = {"land0": 16, "land1": 16}
            with turns(act, 2, t, {**both, "tile": 4, "sg": 4}):
                for u in range(2):
                    s = unit()
                    for m in range(2):
                        gated(sq[:, m, :], s, m, ACT.Sigmoid, used=True)
            with turns(act, 4, t, {**both, "tile": 4, "sg": 2}):
                s = unit()
                for m in range(2):
                    gated(ccs[:, m, :], s, m, ACT.Copy, used=True)
                unit()
                t["tile"].add(2)
            with turns(act, 2, t, {**both, "tile": 4, "val": 4}) as i:
                for u in range(2):
                    unit()
                    for m in range(2):
                        high(bhi[:, bass.ds(4 * i + 2 * u + m, 1), :], sq[:, m, :].unsqueeze(1))
                    t["tile"].add(2)
            with turns(act, 4, t, {**both, "tile": 4, "val": 2}) as i:
                s = unit()
                for m in range(2):
                    gated(ccs[:, m, :], s, m, ACT.Sigmoid)
                unit()
                for m in range(2):
                    high(chi[:, bass.ds(2 * i + m, 1), :], sq[:, m, :].unsqueeze(1))
                t["tile"].add(2)
            with turns(act, 2, t, {**both, "tile": 4}):
                for u in range(2):
                    unit()
                    t["tile"].add(2)
            norm(ahi, modT[:, 3, :])
            with turns(act, 4, t, {"land0": 64, "land1": 64, "tile": 16, "val": 8}):
                for u in range(4):
                    s = unit()
                    for m in range(2):
                        gated(gs[:, m, :], s, m, ACT.Relu)
                        high(hhi[:, 2 * u + m, :], sq[:, m, :])
                for u in range(4):
                    unit()
                    t["tile"].add(2)

            def swiglu(loads_after=1, last=False):
                norm(ahi)

                def slab(pairs, loads_after=1, last=False):
                    for u in range(pairs):
                        s = unit()
                        for m in range(2):
                            gated(gs[:, m, :], s, m, ACT.Silu)
                        unit()
                        for m in range(2):
                            high(hhi[:, 2 * u + m, :], sq[:, m, :])
                        t["tile"].add(2)
                    for u in range(4):
                        if not (last and u == 3):
                            unit(loads_after if u == 3 else 1)
                        t["tile"].add(2)

                with turns(act, 2, t, {"land0": 96, "land1": 96, "tile": 24, "val": 8}):
                    slab(4)
                slab(3, loads_after, last)
                t["x"].add(2 * KB)

            t["x"].add(3 * KB)
            norm()
            swiglu(loads_after=3)

            norm(ahi)

            def fm(dst, b, w=P):
                aux()
                t["fm"].add()
                act.activation(dst, X[b][0:w, :], ACT.Copy).then_inc(fm_ready, 1)
                act.wait_ge(fm_ready, t["fm"].now())
                act.sem_inc(x_free[b], 1)

            unit()
            t["tile"].add(2)
            fm(kaF[:], 0)
            fm(kiF[:], 1)

            def index_relus():
                for n in range(12):
                    aux()
                    q = n % 3 + 1
                    w = (q + 1) * P
                    if t["rl"].local >= 2:
                        act.wait_ge(rl_used, t["rl"].now(-1))
                    t["rl"].add()
                    act.activation(pT[:, n % 2, 0:w], X[2 + n % 2][:, 0:w], ACT.Relu).then_inc(rl_ready, 1)

            for u in range(4):
                unit()
                t["tile"].add(2)
                if u:
                    index_relus()
                for j in range(2):
                    fm(qst[:, j, :], j)
            for u in range(2):
                unit()
                t["tile"].add(2)
                if u == 0:
                    index_relus()
                for j in range(2):
                    fm(qaF[:, 2 * u + j, :], j)
            for u in range(3):
                s = unit()
                w = min(UC, LATB * P - u * UC)
                for half in range(2):
                    tile()
                    link(act.activation(lat[:, 2 * half:2 * half + 2, u * UC:u * UC + w],
                                        G[2 * s + half][:].rearrange("p (b n) -> p b n", b=2)[:, :, 0:w], ACT.Copy))
                    act.sem_inc(g_free[2 * s + half], 1)
            for b in range(TB):
                link(act.activation(sq[:, 0, 0:384], lat[:, b, 0:384], ACT.Square, accum_out=sm1[:, b:b + 1]))
                link(act.activation(sq[:, 0, 0:256], lat[:, b, 384:640], ACT.Square, accum_out=sm1[:, 4 + b:5 + b]))
            link(act.activation(sm1[:, 0:4], sm1[:, 0:4], ACT.Sqrt, bias=epsT[:], scale=1.0 / 384))
            act.activation(sm1[:, 4:8], sm1[:, 4:8], ACT.Sqrt, bias=epsT[:], scale=1.0 / 256).then_inc(lat_ready, 1)
            for j in range(LATB):
                aux()
                act.activation(lhi[:, j, :], X[j % 2][:], ACT.Identity, scale=v3T[:, latg0 + j:latg0 + j + 1])\
                    .then_inc(val_hi, 1)
            for u in range(2):
                unit()
                t["tile"].add(4)
                for j in range(4):
                    fm(qF[:, 4 * u + j, :], j % 2, QH)
            for u in range(2):
                unit()
                t["tile"].add(4)
                for j in range(4):
                    fm(kF[:, 4 * u + j, :], j % 2, QH)
            for latent in range(2):
                with turns(act, NH // 2, t, {"aux": 24, "lg": 8, "pT": 8}):
                    for n in range(10):
                        if n < 8:
                            w = (n % TB + 1) * P
                            t["lg"].add()
                            t["aux"].add()
                            act.wait_ge(lg_ready, t["lg"].now())
                            act.activation(pw[:, n % 2, 0:w], pw[:, n % 2, 0:w], ACT.Exp, bias=sm1[:, n % 2:n % 2 + 1],
                                           accum_out=sm1[:, 8 + n % 2:9 + n % 2]).then_inc(p_ready, 1)
                        if 1 <= n <= 8:
                            w = ((n - 1) % TB + 1) * P
                            aux()
                            t["pT"].add()
                            act.activation(pT[:, (n - 1) % 2, 0:w], X[2][:, 0:w], ACT.Copy).then_inc(pT_ready, 1)
                            act.wait_ge(pT_ready, t["pT"].now())
                            act.sem_inc(x_free[2], 1)
                        if n >= 2:
                            t["aux"].add()
            for k in range(KB):
                aux()
                act.activation(ahi[:, k, :], X[k % 4][:], ACT.Copy).then_inc(val_hi, 1)
            t["val"].add(0)
            for u in range(4):
                unit()
                t["tile"].add(2)
            swiglu(last=True)
            norm()

        @block.gpsimd
        def _(pool):
            pool.memset(ones[:], 1.0).then_inc(gone, 1)
            pool.memset(epsT[:], EPS).then_inc(gone, 1)

        @block.vector
        def _(dve):
            t = Tallies()
            slot = [0]
            tt, ts, stt = dve.tensor_tensor, dve.tensor_scalar, dve.scalar_tensor_tensor

            def unit(last=False):
                s = slot[0]
                if not last:
                    slot[0] ^= 1
                    t["hi"].add()
                    dve.wait_ge(hi_split, t["hi"].now())
                    tt(wlo[s][:], raw[s][:], r32(whi[s][:]), ALU.subtract).then_inc(lo_split, 1)
                return s ^ 1

            def tile():
                t["tile"].add()
                dve.wait_ge(tile_done, t["tile"].now())

            def aux():
                t["aux"].add()
                dve.wait_ge(aux_done, t["aux"].now())

            def link(ins):
                t["step"].add()
                ins.then_inc(dve_step, 1)
                dve.wait_ge(dve_step, t["step"].now())

            def signal(ins, s, name, free=None):
                t[name].add()
                ins.then_inc(s, 1)
                if free is not None:
                    dve.wait_ge(s, t[name].now())
                    dve.sem_inc(free, 1)

            def low(dst, hi, src, bias=None):
                t["vhi"].add()
                t["op"].add()
                dve.wait_ge(val_hi, t["vhi"].now())
                if bias is None:
                    tt(dst, src, r32(hi), ALU.subtract).then_inc(act_ready, 1)
                else:
                    stt(dst, src, bias, r32(hi), ALU.add, ALU.subtract).then_inc(act_ready, 1)

            def add_squares():
                for k in range(1, KB):
                    t["sq"].add(2 if k == 1 else 1)
                    dve.wait_ge(sq_ready, t["sq"].now())
                    if k == 1:
                        tt(ss[:], sq[:, 0, :], sq[:, 1, :], ALU.add).then_inc(ss_added, 1)
                    else:
                        dve.wait_ge(ss_added, t["ss"].now())
                        tt(ss[:], ss[:], sq[:, k % 2, :], ALU.add).then_inc(ss_added, 1)
                    t["ss"].add()

            def invert(b):
                t["rt"].add()
                dve.wait_ge(rt_ready, t["rt"].now())
                dve.sem_inc(x_free[b], 1)
                link(dve.reciprocal(rinv[:], rinv[:]))
                t["aux"].add()

            def norm_split(hi, lo, gain, bias=None):
                add_squares()
                invert(1)
                dve.wait_ge(tile_done, t["tile"].now())

                def value(k):
                    dve.wait_ge(act_ready, t["op"].now())
                    signal(stt(sq[:, k % 2, :], xT[:, k, :], gain[:, k:k + 1], rinv[:], ALU.mult, ALU.mult),
                           val_ready, "val")

                value(0)
                for k in range(KB):
                    if k + 1 < KB:
                        value(k + 1)
                    low(lo[:, k, :], hi[:, k, :], sq[:, k % 2, :], None if bias is None else bias[:, k:k + 1])

            def norm_scale(gain):
                add_squares()
                invert(1)
                for k in range(KB):
                    stt(xT[:, k, :], xT[:, k, :], gain[:, k:k + 1], rinv[:], ALU.mult, ALU.mult).then_inc(x_ready, 1)
                    t["x"].add()

            dve.wait_ge(vec_landed, 16 * VECS)
            dve.tensor_copy(v3[0:XB, :].rearrange("b (r d) -> b r d", r=2),
                            dskip[:].unsqueeze(2).broadcast_to([XB, 2, HEAD_DIM])).then_inc(dskip_ready, 1)
            aux()
            dve.tensor_copy(v2T[:], X[0][:, P:2 * P]).then_inc(vec_ready, 1)
            dve.tensor_copy(v1T[:], X[0][:, 0:P].rearrange("p (j b) -> p j b", j=4))
            link(dve.tensor_copy(v3T[:, 0:VROWS], X[0][:, 2 * P:2 * P + VROWS]))
            dve.sem_inc(x_free[0], 1)
            for k in range(KB):
                tile()
                signal(dve.tensor_copy(xT[:, k, :], G[k % 4][:]), x_ready, "x", g_free[k % 4])
            add_squares()
            invert(1)
            dve.wait_ge(c_ready, 1)

            def ada_unit(buf, acc):
                b = t["ada"].local % 2
                t["ada"].add()
                t[f"al{b}"].add(16)
                dve.wait_ge(ada_landed[b], t[f"al{b}"].now())
                if t["ada"].i is not None or t["ada"].now() > 2:
                    dve.wait_ge(ada_used, t["ada"].now(-2))
                w = unit_view(buf[b])
                link(ts(acc[:, b, :], w[:, 0, :], cact[:, 0:1], None, ALU.mult))
                for k in range(1, KB - 1):
                    link(stt(acc[:, b, :], w[:, k, :], cact[:, k:k + 1], acc[:, b, :], ALU.mult, ALU.add))
                stt(acc[:, b, :], w[:, KB - 1, :], cact[:, KB - 1:KB], acc[:, b, :], ALU.mult, ALU.add)\
                    .then_inc(ada_acc, 1)

            def unit_view(buf):
                return buf[:, :].rearrange("p (k n) -> p k n", k=KB)

            for u in range(8):
                ada_unit(araw, adacc)
            dve.wait_ge(ada_used, 8)
            link(tt(modT[:, 0:2, :], X[3][:, 0:16].rearrange("p (j k) -> p j k", k=KB),
                    badaT[:, 0:16].rearrange("p (j k) -> p j k", k=KB), ALU.add))
            dve.sem_inc(x_free[3], 1)
            link(stt(coef[:], modT[:, 1, :], 1.0, ln1T, ALU.add, ALU.mult))
            t["hi"].add()
            dve.wait_ge(hi_split, t["hi"].now())
            n0 = KB * HEADS
            tt(wlo[0][:, 0:n0], raw[0][:, 0:n0], r32(whi[0][:, 0:n0]), ALU.subtract).then_inc(lo_split, 1)
            slot[0] = 1

            def value(k):
                if k >= 2:
                    dve.wait_ge(act_ready, t["op"].now())
                signal(stt(sq[:, k % 2, :], xT[:, k, :], coef[:, k:k + 1], rinv[:], ALU.mult, ALU.mult),
                       val_ready, "val")

            value(0)
            for k in range(KB):
                if k + 1 < KB:
                    value(k + 1)
                low(alo[:, k, :], ahi[:, k, :], sq[:, k % 2, :], modT[:, 0, k:k + 1])
            link(dve.memset(pacc[:], 0.0))
            link(dve.memset(pre[:, :, 0:3], 0.0))

            unit()
            tile()
            dve.wait_ge(vec_landed, 16 * VECS)
            heads = lambda kind: dts[:, kind]
            over = lambda j: dtw[:, j, :].unsqueeze(1).broadcast_to([P, TB, HEADS])
            tt(heads(TMP), G[0][:, 0:P].rearrange("p (c h) -> p c h", c=TB), over(0), ALU.add).then_inc(prep_v, 1)
            dve.wait_ge(prep_v, 1)
            dve.sem_inc(g_free[0], 1)
            dve.wait_ge(prep_a, 1)
            ts(heads(AC), heads(DT), 1.0, None, ALU.add).then_inc(prep_v, 1)
            dve.wait_ge(prep_v, 2)
            link(ts(heads(TOEND), heads(AC), -1.0, None, ALU.add))
            link(ts(heads(EEND), heads(TOEND), 0.0, None, ALU.is_equal))
            link(tt(heads(TOEND), heads(TOEND), heads(EEND), ALU.add))
            link(dve.reciprocal(heads(TOEND), heads(TOEND)))
            link(tt(heads(TOEND), heads(TOEND), heads(DT), ALU.mult))
            dve.wait_ge(prep_a, 2)
            link(tt(heads(TOEND), heads(TOEND), heads(EAC), ALU.mult))
            link(tt(heads(EEND), heads(EEND), heads(DT), ALU.mult))
            link(tt(heads(TOEND), heads(TOEND), heads(EEND), ALU.add))
            link(stt(heads(DT), heads(TMP), 0.0, heads(TOEND), ALU.max, ALU.add))
            stt(heads(TMP), heads(DT), -1.0, over(1), ALU.mult, ALU.mult).then_inc(prep_v, 1)

            def convs(first, blks, bank):
                steps = []
                for m, blk in zip((first, first + 1), blks):
                    t["pre"].add()
                    seen = t["pre"].local

                    def step(j, m=m, blk=blk, seen=seen):
                        if j == 0:
                            dve.wait_ge(pre_ready, t["pre"].now(seen - t["pre"].local))
                            dve.sem_inc(g_free[bank + m - first], 1)
                        ins = stt(cv[:, m, :], pre[:, m, j:j + T], v1T[:, j, bass.ds(blk, 1)], cv[:, m, :],
                                  ALU.mult, ALU.add)
                        if j < 2:
                            link(ins)
                        else:
                            ins.then_inc(cv_ready, 1)

                    steps += [lambda j=j, step=step: step(j) for j in range(3)]
                return steps

            def group_heads(kind, c0, c1, g):
                v = dts[:, kind, c0:c1, bass.ds(g * RH, RH)]
                return v.unsqueeze(3).broadcast_to([P, c1 - c0, RH, HEAD_DIM])

            def by_head(ap):
                return ap.rearrange("p c (r d) -> p c r d", r=RH)

            def two(bank):
                return bank[:].rearrange("p (c r d) -> p c r d", c=2, r=RH)

            def scan_turn(g, gemm, ssd, outp):
                q = g - 1
                steps = []
                if gemm:
                    s = unit()
                    t["tile"].add(2)
                if outp:
                    t["sq"].add(2)
                    dve.wait_ge(sq_ready, t["sq"].now())
                    signal(tt(ss[:], sq[:, 0, :], sq[:, 1, :], ALU.add), ss_added, "ss")
                    invert(2)
                    for b in range(2):
                        signal(stt(sq[:, b, :], yf[:, b, :], v3T[:, bass.ds(normw0 + 2 * (g - 2) + b, 1)], rinv[:],
                                   ALU.mult, ALU.mult), val_ready, "val")
                    for b in range(2):
                        low(ylo[:, b, :], yhi[:, b, :], sq[:, b, :])
                if gemm:
                    steps = convs(0, (2 * g, 2 * g + 1), 2 * s)
                if outp:
                    so = unit()
                    for m in range(KB):
                        tile()
                        tt(pacc[:, m, :], pacc[:, m, :], G[2 * so + m % 2][:], ALU.add)\
                            .then_inc(g_free[2 * so + m % 2], 1)
                        if steps:
                            steps.pop(0)()
                for step in steps:
                    step()
                if gemm:
                    s = unit()
                if ssd:
                    for half in range(2):
                        aux()
                        tt(by_head(xdt[:, 2 * half:2 * half + 2, :]), two(X[half]),
                           group_heads(DT, 2 * half, 2 * half + 2, q), ALU.mult).then_inc(x_free[half], 1)
                    t["aux"].add()
                    aux()
                    tt(sm[:], X[3][:].rearrange("p (c n) -> p c n", c=TB),
                       triu[:].unsqueeze(1).broadcast_to([P, TB, P]), ALU.mult).then_inc(x_free[3], 1)
                    t["bc"].add(16)
                    dve.wait_ge(bc_landed, t["bc"].now())
                    for r in range(RH):
                        for c in range(TB):
                            last = ts(seg[:, r, c * P:(c + 1) * P], bc[:, r, c * P:(c + 1) * P],
                                      dts[:, AC, c, bass.ds(q * RH + r, 1)], 0.0, ALU.subtract, ALU.min)
                        last.then_inc(seg_ready, 1)
                    t["exp"].add()
                    for r in range(RH):
                        dve.wait_ge(exp_ready, t["exp"].now(r))
                        if r == 0:
                            tt(by_head(xw[:]), by_head(xdt[:]), group_heads(TOEND, 0, TB, q), ALU.mult)\
                                .then_inc(xw_ready, 1)
                        tt(seg[:, r, :], seg[:, r, :], sm[:].rearrange("p c n -> p (c n)"), ALU.mult)\
                            .then_inc(m_ready, 1)
                    t["exp"].add(RH - 1)
                if gemm:
                    sb = s
                    t["tile"].add(2)
                    unit()
                if ssd:
                    t["aux"].add()
                    aux()
                    link(dve.tensor_copy(states[:, 0, :], X[2][:, 0:GW]))
                    for c in (1, 2):
                        link(tt(states[:, c, :].rearrange("p (r d) -> p r d", r=RH),
                                states[:, c - 1, :].rearrange("p (r d) -> p r d", r=RH),
                                dts[:, EEND, c, bass.ds(q * RH, RH)].unsqueeze(2).broadcast_to([P, RH, HEAD_DIM]),
                                ALU.mult))
                        src = X[2][:, GW:2 * GW] if c == 1 else X[3][:, 0:GW]
                        ins = tt(states[:, c, :], states[:, c, :], src, ALU.add)
                        if c == 1:
                            link(ins)
                            dve.sem_inc(x_free[2], 1)
                        else:
                            signal(ins, st_ready, "st", x_free[3])
                if gemm:
                    for step in convs(2, (XB + g, XB + GROUPS + g), 2 * sb):
                        step()
                if ssd:
                    aux()
                    link(tt(by_head(ytok[:, 1:3, :]), two(X[2]), group_heads(EAC, 1, 3, q), ALU.mult))
                    dve.sem_inc(x_free[2], 1)
                    link(tt(by_head(ytok[:, 3:4, :]), X[3][:, 0:GW].rearrange("p (c r d) -> p c r d", c=1, r=RH),
                            group_heads(EAC, 3, 4, q), ALU.mult))
                    dve.sem_inc(x_free[3], 1)
                    dve.tensor_copy(ytok[:, 0, :], X[0][:, 0:GW])
                    tt(ytok[:, 1, :], ytok[:, 1, :], X[0][:, GW:2 * GW], ALU.add).then_inc(x_free[0], 1)
                    signal(tt(ytok[:, 2:4, :], ytok[:, 2:4, :], X[1][:].rearrange("p (c n) -> p c n", c=2), ALU.add),
                           ytok_ready, "yt", x_free[1])
                    for b in range(2):
                        aux()
                        link(stt(yf[:, b, :], xf[:, b, :], v3T[:, bass.ds(dskip0 + 2 * q + b, 1)], X[b][:],
                                 ALU.mult, ALU.add))
                        dve.sem_inc(x_free[b], 1)
                        tt(yf[:, b, :], yf[:, b, :], zs[:, b, :], ALU.mult).then_inc(yf_ready, 1)
                if gemm:
                    t["tile"].add(2)

            scan_turn(0, True, False, False)
            aux()
            link(dve.tensor_copy(heads(AC), X[0][:, 0:P].rearrange("p (c h) -> p c h", c=TB)))
            aux()
            tt(heads(TOEND), X[1][:, 0:P].rearrange("p (c h) -> p c h", c=TB), heads(AC), ALU.subtract)\
                .then_inc(prep_v, 1)
            t["aux"].add()
            dve.wait_ge(prep_a, 3)
            for b in range(3):
                dve.sem_inc(x_free[b], 1)
            scan_turn(1, True, True, False)
            with turns(dve, GROUPS - 2, t, {"hi": 4, "tile": 14, "aux": 10, "sq": 2, "ss": 1, "rt": 1, "val": 2,
                                            "vhi": 2, "op": 2, "pre": 4, "bc": 16, "exp": 4, "st": 1, "yt": 1, "step": 17}) as i:
                scan_turn(i + 2, True, True, True)
            scan_turn(GROUPS, False, True, True)
            scan_turn(GROUPS + 1, False, False, True)

            def gate_used(s, m):
                t["tile"].add()
                t["sg"].add()
                dve.wait_ge(sg_ready, t["sg"].now())
                dve.sem_inc(g_free[2 * s + m], 1)

            with turns(dve, 2, t, {"hi": 2, "tile": 4, "sg": 4, "ada": 2, "al0": 16, "al1": 16, "step": 14}) as i:
                for u in range(2):
                    s = unit()
                    for m in range(2):
                        gate_used(s, m)
                        dst = pacc[:, bass.ds(4 * i + 2 * u + m, 1), :]
                        tt(dst, dst, sq[:, m, :].unsqueeze(1), ALU.mult).then_inc(sg_used, 1)
                for u in range(2):
                    ada_unit(braw, badacc)
            link(dve.memset(pb[:, :, 0:2], 0.0))
            t["used"].add(8)
            with turns(dve, 4, t, {"hi": 2, "tile": 4, "sg": 2, "ada": 2, "al0": 16, "al1": 16, "step": 20,
                                   "used": 2}) as i:
                s = unit()
                for m in range(2):
                    gate_used(s, m)
                s = unit()
                for m in range(2):
                    tile()
                    signal(tt(pb[:, m, 2:2 + T], G[2 * s + m][:], ccs[:, m, :], ALU.mult), sg_used, "used",
                           g_free[2 * s + m])
                    dst = qc[:, bass.ds(2 * i + m, 1), :]
                    link(ts(dst, pb[:, m, 2:2 + T].unsqueeze(1), v2T[:, bass.ds(convw0 + 2 * KB + 2 * i + m, 1)], None,
                            ALU.mult))
                    for j in (1, 0):
                        link(stt(dst, pb[:, m, j:j + T].unsqueeze(1), v2T[:, bass.ds(convw0 + j * KB + 2 * i + m, 1)],
                                 dst, ALU.mult, ALU.add))
                for u in range(2):
                    ada_unit(braw, badacc)
            with turns(dve, 2, t, {"hi": 2, "tile": 4, "val": 4, "vhi": 4, "op": 4, "ada": 2, "al0": 16, "al1": 16,
                                   "step": 14}) as i:
                for u in range(2):
                    s = unit()
                    for m in range(2):
                        tile()
                        k = bass.ds(4 * i + 2 * u + m, 1)
                        signal(tt(sq[:, m, :].unsqueeze(1), G[2 * s + m][:].unsqueeze(1), qc[:, k, :], ALU.mult),
                               val_ready, "val", g_free[2 * s + m])
                        low(blo[:, k, :], bhi[:, k, :], sq[:, m, :].unsqueeze(1))
                for u in range(2):
                    ada_unit(braw, badacc)
            dve.wait_ge(ada_used, 24)
            link(tt(modT[:, 2:6, :], X[3][:, 16:48].rearrange("p (j k) -> p j k", k=KB),
                    badaT[:, 16:48].rearrange("p (j k) -> p j k", k=KB), ALU.add))
            dve.sem_inc(x_free[3], 1)
            link(stt(coef[:], modT[:, 4, :], 1.0, ln2T, ALU.add, ALU.mult))
            with turns(dve, 4, t, {"hi": 2, "tile": 4, "sg": 2, "val": 2, "vhi": 2, "op": 2, "step": 2}) as i:
                s = unit()
                for m in range(2):
                    gate_used(s, m)
                s = unit()
                for m in range(2):
                    tile()
                    k = bass.ds(2 * i + m, 1)
                    link(tt(sq[:, m, :], G[2 * s + m][:], ccs[:, m, :], ALU.mult))
                    dve.sem_inc(g_free[2 * s + m], 1)
                    signal(tt(sq[:, m, :].unsqueeze(1), sq[:, m, :].unsqueeze(1), pacc[:, k, :], ALU.add),
                           val_ready, "val")
                    low(clo[:, k, :], chi[:, k, :], sq[:, m, :].unsqueeze(1))

            def residual(s, m, k, gain):
                tile()
                dst = xT[:, k, :]
                src = G[2 * s + m][:].unsqueeze(1)
                signal(stt(dst, src, gain, dst, ALU.mult, ALU.add), x_ready, "x", g_free[2 * s + m])

            with turns(dve, 2, t, {"hi": 2, "tile": 4, "x": 4}) as i:
                for u in range(2):
                    s = unit()
                    for m in range(2):
                        residual(s, m, bass.ds(4 * i + 2 * u + m, 1), modT[:, 2, bass.ds(4 * i + 2 * u + m, 1)])
            norm_split(ahi, alo, coef, modT[:, 3, :])
            with turns(dve, 4, t, {"hi": 8, "tile": 16, "sg": 8, "val": 8, "vhi": 8, "op": 8, "x": 8}):
                for u in range(4):
                    s = unit()
                    for m in range(2):
                        gate_used(s, m)
                        signal(tt(sq[:, m, :], gs[:, m, :], gs[:, m, :], ALU.mult), val_ready, "val")
                        low(hlo[:, 2 * u + m, :], hhi[:, 2 * u + m, :], sq[:, m, :])
                for u in range(4):
                    s = unit()
                    for m in range(2):
                        residual(s, m, slice(2 * u + m, 2 * u + m + 1), modT[:, 5, 2 * u + m:2 * u + m + 1])

            def swiglu(gain, last=False):
                norm_split(ahi, alo, gain)

                def slab(pairs, last=False):
                    for u in range(pairs):
                        s = unit()
                        for m in range(2):
                            gate_used(s, m)
                        s = unit()
                        for m in range(2):
                            tile()
                            signal(tt(sq[:, m, :], gs[:, m, :], G[2 * s + m][:], ALU.mult), val_ready, "val",
                                   g_free[2 * s + m])
                            low(hlo[:, 2 * u + m, :], hhi[:, 2 * u + m, :], sq[:, m, :])
                    for u in range(4):
                        s = unit(last and u == 3)
                        for m in range(2):
                            residual(s, m, slice(2 * u + m, 2 * u + m + 1), 0.5)

                with turns(dve, 2, t, {"hi": 12, "tile": 24, "sg": 8, "val": 8, "vhi": 8, "op": 8, "x": 8}):
                    slab(4)
                slab(3, last)

            norm_scale(finalT)
            swiglu(gf1T)

            norm_split(ahi, alo, gmixT)

            def rope(dst, src, tmp, tab, half, w):
                heads = src.shape[2]
                h = w // 2

                def row(j, lo, hi):
                    return tab[:, j, 2 * half:2 * half + 2, lo:hi].unsqueeze(2).broadcast_to([P, 2, heads, hi - lo])

                tt(dst, src, row(0, 0, w), ALU.mult)
                tt(tmp[:, :, :, 0:h], src[:, :, :, h:w], row(1, 0, h), ALU.mult)
                link(tt(tmp[:, :, :, h:w], src[:, :, :, 0:h], row(1, h, w), ALU.mult))
                link(tt(dst, dst, tmp, ALU.add))

            def tmp4(heads, w):
                return rtmp[:, 0:2 * heads * w].rearrange("p (b h d) -> p b h d", b=2, h=heads)

            s = unit()
            dve.wait_ge(tab_landed, 16 * 5)
            link(dve.memset(score[:], 0.0))
            link(dve.memset(biasM[:, 0:T - P], 0.0))
            link(dve.tensor_copy(biasM[:, T - P:T], nmask[:]))
            link(dve.tensor_copy(bias[:, 0:P], nmask[:]))
            for half in range(2):
                tile()
                b2 = slice(2 * half, 2 * half + 2)
                src = G[2 * s + half][:].rearrange("p (b n) -> p b n", b=2)
                for dst, at in ((kk, 0), (qtok, M_KI)):
                    rope(dst[:, b2, 0:HD].unsqueeze(2), src[:, :, at:at + HD].unsqueeze(2), tmp4(1, HD), tab64, half, HD)
                    link(dve.tensor_copy(dst[:, b2, HD:2 * HD], dst[:, b2, 0:HD]))
                rope(krt[:, b2, :].unsqueeze(2), src[:, :, M_KR:M_KR + ROPE].unsqueeze(2), tmp4(1, ROPE), tab32, half,
                     ROPE)
                link(dve.tensor_copy(va[:, b2, :], src[:, :, M_VA:M_VA + HD]))
                signal(ts(wix[:, b2, :], src[:, :, M_WI:M_WI + IDX_HEADS], 1.0 / 32.0, None, ALU.mult),
                       k_ready, "k", g_free[2 * s + half])
            t["aux"].add(2)

            def rope_unit():
                s = unit()
                if t["aux"].now():
                    dve.wait_ge(aux_done, t["aux"].now())
                for half in range(2):
                    tile()
                    b2 = slice(2 * half, 2 * half + 2)
                    rope(qtok[:, b2, 0:UC].rearrange("p b (h d) -> p b h d", h=4),
                         G[2 * s + half][:].rearrange("p (b h d) -> p b h d", b=2, h=4), tmp4(4, HD), tab64, half, HD)
                    if half == 0:
                        dve.sem_inc(g_free[2 * s], 1)
                dve.sem_inc(g_free[2 * s + 1], 1)
                dve.sem_inc(k_ready, 1)
                t["k"].add()

            def index_sums(u):
                for n in range(12):
                    h, q = 4 * u + n // 3, n % 3 + 1
                    t["aux"].add()
                    t["rl"].add()
                    dve.wait_ge(rl_ready, t["rl"].now())
                    dve.sem_inc(x_free[2 + n % 2], 1)
                    w = (q + 1) * P
                    dst = score[:, SOFF[q]:SOFF[q] + w]
                    if n >= 3:
                        dve.wait_ge(rl_used, t["rl"].now(-3))
                    stt(dst, pT[:, n % 2, 0:w], wix[:, q, h:h + 1], dst, ALU.mult, ALU.add).then_inc(rl_used, 1)

            def search():
                dve.wait_ge(rl_used, t["rl"].now())
                for q in range(1, TB):
                    w = (q + 1) * P
                    mine = score[:, SOFF[q]:SOFF[q] + w]
                    link(tt(mine[:, q * P:w], mine[:, q * P:w], nmask[:], ALU.add))
                    for _ in range(TOPK // 8):
                        link(dve.max(m8[:], mine))
                        link(dve.match_replace(mine, m8[:], mine, TAKEN))
                        yield
                    link(ts(bias[:, BOFF[q]:BOFF[q] + w], mine, TAKEN / 2, NEG, ALU.is_gt, ALU.mult))

            rounds = search()

            def some_rounds(n):
                for _ in range(n):
                    next(rounds, None)

            for u in range(4):
                rope_unit()
                if u:
                    index_sums(u - 1)
                t["aux"].add(2)
            for u in range(2):
                rope_unit()
                if u == 0:
                    index_sums(3)
                t["aux"].add(2)
                some_rounds(4)
            for u in range(3):
                unit()
                t["tile"].add(2)
                some_rounds(6)
            dve.wait_ge(lat_ready, 1)
            link(dve.reciprocal(sm1[:, 0:8], sm1[:, 0:8]))
            for b in range(TB):
                ts(lat[:, b, 0:384], lat[:, b, 0:384], sm1[:, b:b + 1], None, ALU.mult)
                last = ts(lat[:, b, 384:640], lat[:, b, 384:640], sm1[:, 4 + b:5 + b], None, ALU.mult)
            last.then_inc(lat_done, 1)
            for j in range(LATB):
                t["vhi"].add()
                t["aux"].add()
                dve.wait_ge(val_hi, t["vhi"].now())
                link(stt(llo[:, j, :], X[j % 2][:], v3T[:, latg0 + j:latg0 + j + 1], r32(lhi[:, j, :]), ALU.mult,
                         ALU.subtract))
                t["op"].add()
                dve.sem_inc(act_ready, 1)
                dve.sem_inc(x_free[j % 2], 1)

            def heads96(b):
                return qtok[:, b, :].rearrange("p (h d) -> p h d", h=4)

            def rope96(dst, src, b):
                h = ROPE // 2
                tmp = rtmp[:, 0:4 * ROPE].rearrange("p (h d) -> p h d", h=4)

                def row(j, lo, hi):
                    return tab32[:, j, b, lo:hi].unsqueeze(1).broadcast_to([P, 4, hi - lo])

                tt(dst, src, row(0, 0, ROPE), ALU.mult)
                tt(tmp[:, :, 0:h], src[:, :, h:ROPE], row(1, 0, h), ALU.mult)
                link(tt(tmp[:, :, h:ROPE], src[:, :, 0:h], row(1, h, ROPE), ALU.mult))
                link(tt(dst, dst, tmp, ALU.add))

            for u in range(2):
                s = unit()
                dve.wait_ge(aux_done, t["aux"].now())
                for b in range(TB):
                    tile()
                    src = G[2 * s + b % 2][:, 0:4 * QH].rearrange("p (h d) -> p h d", h=4)
                    link(dve.tensor_copy(heads96(b)[:, :, 0:HD], src[:, :, 0:HD]))
                    rope96(heads96(b)[:, :, HD:QH], src[:, :, HD:QH], b)
                    dve.sem_inc(g_free[2 * s + b % 2], 1)
                dve.sem_inc(k_ready, 1)
                t["aux"].add(4)
                some_rounds(7)
            for u in range(2):
                s = unit()
                dve.wait_ge(aux_done, t["aux"].now())
                for b in range(TB):
                    tile()
                    src = G[2 * s + b % 2][:].rearrange("p (h d) -> p h d", h=4)
                    dve.tensor_copy(heads96(b)[:, :, 0:HD], src[:, :, 0:HD])
                    dve.tensor_copy(heads96(b)[:, :, HD:QH], krt[:, b, :].unsqueeze(1).broadcast_to([P, 4, ROPE]))
                    link(dve.tensor_copy(vt[:, b, 4 * HD * u:4 * HD * (u + 1)].rearrange("p (h d) -> p h d", h=4),
                                         src[:, :, HD:2 * HD]))
                    dve.sem_inc(g_free[2 * s + b % 2], 1)
                dve.sem_inc(k_ready, 1)
                t["aux"].add(4)
                some_rounds(7)
            some_rounds(100)

            for latent in range(2):
                scale = QH ** -0.5 if latent else HD ** -0.5
                with turns(dve, NH // 2, t, {"aux": 24, "lg": 8, "pr": 8, "step": 24}) as i:
                    for n in range(10):
                        if n < 8:
                            q = n % TB
                            w = (q + 1) * P
                            aux()
                            mask = biasM[:, T - w:T] if latent else bias[:, BOFF[q]:BOFF[q] + w]
                            link(stt(pw[:, n % 2, 0:w], X[n % 2][:, 0:w], scale, mask, ALU.mult, ALU.add))
                            dve.sem_inc(x_free[n % 2], 1)
                            t["lg"].add()
                            dve.tensor_reduce(sm1[:, n % 2:n % 2 + 1], pw[:, n % 2, 0:w], AX_X, ALU.max, negate=True)\
                                .then_inc(lg_ready, 1)
                        if 1 <= n <= 8:
                            t["aux"].add()
                            t["pr"].add()
                            dve.wait_ge(p_ready, t["pr"].now())
                            m = (n - 1) % 2
                            link(dve.reciprocal(sm1[:, 10 + m:11 + m], sm1[:, 8 + m:9 + m]))
                        if n >= 2:
                            aux()
                            m = n % 2
                            q = (n - 2) % TB
                            at = latent * T + (2 * i + (n - 2) // TB) * HD
                            link(ts(otok[:, q, bass.ds(at, HD)], X[3][:, 0:HD], sm1[:, 10 + m:11 + m], None, ALU.mult))
                            dve.sem_inc(x_free[3], 1)
            dve.sem_inc(o_ready, 1)
            for k in range(KB):
                t["vhi"].add()
                t["aux"].add()
                dve.wait_ge(val_hi, t["vhi"].now())
                link(tt(alo[:, k, :], X[k % 4][:], r32(ahi[:, k, :]), ALU.subtract))
                t["op"].add()
                dve.sem_inc(act_ready, 1)
                dve.sem_inc(x_free[k % 4], 1)
            for u in range(4):
                s = unit()
                for m in range(2):
                    residual(s, m, slice(2 * u + m, 2 * u + m + 1), 1.0)
            swiglu(gf2T, last=True)
            norm_scale(gfinT)
            for n in range(2 * TB):
                aux()
                bank = 2 * ((n // 2) % 2) + n % 2
                signal(dve.tensor_copy(xout[:, n // 2, (n % 2) * T:(n % 2 + 1) * T], X[bank][:]), o_copied, "oc",
                       x_free[bank])


INPUTS = ("x", "c", "w_ada", "b_ada", "ln1", "ln2", "w_in", "conv_w", "ssm_conv_w", "ssm_conv_b", "dt_bias",
          "a_log", "d_skip", "ssm_norm_w", "w_conv_out", "w_ssm_out", "w_o", "w_up", "w_down", "final_norm",
          "g_ffn1_2", "w1_gate_2", "w1_up_2", "w1_down_2", "g_mix_2", "w_in_2", "g_q_lat_2", "g_kv_lat_2",
          "w_uq_2", "w_ukv_2", "w_out_2", "g_ffn2_2", "w2_gate_2", "w2_up_2", "w2_down_2", "g_final_2")


def constants():
    def rotary(dim):
        pos = np.arange(T, dtype=np.float32)
        inv = np.float32(10000.0) ** (-np.arange(0, dim, 2, dtype=np.float32) / np.float32(dim))
        ang = pos[:, None] * inv[None, :].astype(np.float32)
        cos, sin = np.cos(ang).astype(np.float32), np.sin(ang).astype(np.float32)
        return np.concatenate([cos, cos], 1), np.concatenate([-sin, sin], 1)

    cos64, sin64 = rotary(HD)
    cos32, sin32 = rotary(ROPE)
    row = np.arange(P)
    return {
        "ident": np.eye(P, dtype=np.float32),
        "triu": (row[:, None] <= row[None, :]).astype(np.float32),
        "nmask": np.where(row[None, :] <= row[:, None], 0.0, NEG).astype(np.float32),
        "cos64": cos64, "sin64": sin64, "cos32": cos32, "sin32": sin32,
    }


def kernel(**inputs):
    import concourse.bacc as bacc
    from concourse.bass_utils import run_bass_kernel_spmd

    nc = bacc.Bacc("TRN2", target_bir_lowering=False, num_devices=1)
    arrays, aps = {}, {}
    given = {name: inputs[name] for name in INPUTS}
    for name, value in {**given, **constants()}.items():
        value = np.ascontiguousarray(value)
        arrays[f"in_{name}"] = value
        aps[name] = nc.dram_tensor(f"in_{name}", value.shape, mybir.dt.from_np(value.dtype), kind="ExternalInput").ap()
    out = nc.dram_tensor("out_x", (1, T, D), F32, kind="ExternalOutput").ap()
    build(nc, aps, out)
    result = run_bass_kernel_spmd(nc, [arrays], core_ids=[0])
    return result.results[0]["out_x"]
```

```python
from contextlib import ExitStack, contextmanager

import numpy as np

import concourse.bass as bass
from concourse import mybir

F32 = mybir.dt.float32
F32R = mybir.dt.float32r
ALU = mybir.AluOpType
ACT = mybir.ActivationFunctionType
AX_X = mybir.AxisListType.X

P = 128
T = 512
TB = T // P
D = 1024
KB = D // P
UC = 256
UNIT = KB * UC
EPS = 1e-6
NEG = -1e30
TAKEN = -3e38

HEADS, HEAD_DIM = 32, 64
D_SSM = HEADS * HEAD_DIM
GROUPS, STATE = 8, 128
RH = HEADS // GROUPS
GW = RH * HEAD_DIM
CONV_BLOCKS = (D_SSM + 2 * GROUPS * STATE) // P
XB = D_SSM // P
C_GL, C_CB, C_CC, C_CX, C_Z = 0, 2 * D, 3 * D, 4 * D, 5 * D
C_X = C_Z + D_SSM
C_B = C_X + D_SSM
C_C = C_B + GROUPS * STATE
C_DT = C_C + GROUPS * STATE
D_FF = 4 * D
D_FF_2 = 2816
NH, HD = 8, 64
IDX_HEADS = 16
TOPK = 128
ROPE = 32
QH = HD + ROPE
LATB = 5
C_KA, C_QI, C_KI, C_LAT, C_KR = 512, 640, 1664, 1744, 2384
M_VA, M_KI, M_WI, M_KR, M_W = 64, 128, 192, 208, 240
TILES_START = KB
TILES_SCAN = TILES_START + 1 + GROUPS * (6 + 8)
TILES_BEFORE_MIX2 = TILES_SCAN + 8 + 24 + 16 + 8 + 64 + 68
VECS, VROWS = 25, 77
FIRST_ON_PE = (0, 4)
XREADY_END = 8 + 8 + 32 + 8 + 24 + 8 + 24 + 8
FM_ALL = 2 + 8 + 4 + 8 + 8
SOFF = {1: 0, 2: 256, 3: 640}
BOFF = {0: 0, 1: 128, 2: 384, 3: 768}


class Tally:

    def __init__(self, name):
        self.name, self.base, self.per, self.i, self.local = name, 0, 0, None, 0

    def add(self, n=1):
        self.local += n

    def now(self, more=0):
        v = self.base + self.local + more
        return v + self.per * self.i if self.i is not None and self.per else v


class Tallies:

    def __init__(self):
        self.all = {}

    def __getitem__(self, name):
        if name not in self.all:
            self.all[name] = Tally(name)
        return self.all[name]


@contextmanager
def turns(eng, n, tallies, per):
    for name in per:
        tallies[name]
    with eng.Fori(0, n) as i:
        for t in tallies.all.values():
            t.base, t.local, t.i, t.per = t.base + t.local, 0, i, per.get(t.name, 0)
        yield i
    wrong = {t.name: t.local for t in tallies.all.values() if t.local != t.per}
    assert not wrong, f"a turn moves {wrong}"
    for t in tallies.all.values():
        t.base, t.local, t.i, t.per = t.base + t.per * n, 0, None, 0


def r32(ap):
    return ap.bitcast(F32)


def build(nc, a, out):
    ctx = ExitStack()
    with ctx:
        def sem(name):
            return ctx.enter_context(nc.semaphore(name))

        def fixed(name, shape, dt=F32):
            return ctx.enter_context(nc.sbuf_tensor(name, shape, dt))

        raw = [fixed(f"raw{s}", [P, UNIT]) for s in range(2)]
        whi = [fixed(f"whi{s}", [P, UNIT], F32R) for s in range(2)]
        wlo = [fixed(f"wlo{s}", [P, UNIT], F32R) for s in range(2)]
        xT = fixed("xT", [P, KB, T])
        sq = fixed("sq", [P, 2, T])
        ss = fixed("ss", [P, T])
        rinv = fixed("rinv", [P, T])
        ident = fixed("ident", [P, P])
        triu = fixed("triu", [P, P])
        ones = fixed("ones", [P, P])
        v1 = fixed("v1", [P, P])
        v2 = fixed("v2", [P, P])
        v3 = fixed("v3", [P, P])
        v1T = fixed("v1T", [P, 4, CONV_BLOCKS])
        v2T = fixed("v2T", [P, P])
        v3T = fixed("v3T", [P, P])
        cact = fixed("cact", [P, KB])
        modT = fixed("modT", [P, 6, KB])
        coef = fixed("coef", [P, KB])
        epsT = fixed("epsT", [P, 1])
        dskip = fixed("dskip", [XB, 2])
        warm = fixed("warm", [P, 1])
        ln1T, ln2T = v2T[:, 0:8], v2T[:, 8:16]
        badaT, cT = v2T[:, 16:64], v2T[:, 64:72]
        convb0, convw0 = 72, 104
        finalT, gf1T, gmixT, gf2T, gfinT = (v3T[:, 32 + 8 * j:40 + 8 * j] for j in range(5))
        dskip0, normw0, latg0 = 0, 16, 72

        G = [ctx.enter_context(nc.psum_tensor(f"G{b}", [P, T], F32)) for b in range(4)]
        X = [ctx.enter_context(nc.psum_tensor(f"X{b}", [P, T], F32)) for b in range(4)]

        def phase(*specs):
            with ExitStack() as st:
                return [st.enter_context(nc.sbuf_tensor(s[0], s[1], s[2] if len(s) > 2 else F32)) for s in specs]

        split_a = (("ahi", [P, KB, T], F32R), ("alo", [P, KB, T], F32R))

        def after_a(tag, *specs):
            return phase(*((n + tag, s, d) for n, s, d in split_a), *specs)[2:]

        ahi, alo, xin, *araw = phase(*split_a, ("xin", [P, TB, D]), *((f"araw{u}", [P, UNIT]) for u in range(8)),
                                     ("adacc", [P, 2, UC]))
        adacc = araw.pop()
        (pacc, pre, cv, xf, zs, xdt, xw, btok, sm, seg, bc, states, yf, yhi, ylo, dts, dtw) = after_a(
            "_s", ("pacc", [P, KB, T]), ("pre", [P, 4, 3 + T]), ("cv", [P, 4, T]), ("xf", [P, 4, T]),
            ("zs", [P, 2, T]), ("xdt", [P, TB, GW]), ("xw", [P, TB, GW]), ("btok", [P, TB, P]),
            ("sm", [P, TB, P]), ("seg", [P, RH, T]), ("bc", [P, RH, T]), ("states", [P, 3, GW]),
            ("yf", [P, 2, T]), ("yhi", [P, 2, T], F32R), ("ylo", [P, 2, T], F32R),
            ("dts", [P, 6, TB, HEADS]), ("dtw", [P, 2, HEADS]))
        ytok = xw
        acT = ss
        DT, AC, EAC, TOEND, EEND, TMP = range(6)
        (_, bhi, blo, qc, braw0, braw1, ccs, pb, badacc) = after_a(
            "_c", ("pacc_c", [P, KB, T]), ("bhi", [P, KB, T], F32R), ("blo", [P, KB, T], F32R),
            ("qc", [P, KB, T]), ("braw0", [P, UNIT]), ("braw1", [P, UNIT]),
            ("ccs", [P, 2, T]), ("pb", [P, 2, 2 + T]), ("badacc", [P, 2, UC]))
        braw = [braw0, braw1]
        (_, _, _, chi, clo) = after_a(
            "_m", ("pacc_m", [P, KB, T]), ("bhi_m", [P, KB, T], F32R), ("blo_m", [P, KB, T], F32R),
            ("chi", [P, KB, T], F32R), ("clo", [P, KB, T], F32R))
        (hhi, hlo, gs, rr, gf) = after_a("_f", ("hhi", [P, KB, T], F32R), ("hlo", [P, KB, T], F32R), ("gs", [P, 2, T]),
                                     ("rr", [P, T]), ("gf", [P, KB]))
        (qF, kF, otok, _, qaF, kaF, kiF, va, wix, krt, kk, score, bias, tab64, tab32, qtok, rtmp, lat, vt, qst,
         pT, biasM, nmask, sm1, m8) = phase(
            ("qF", [QH, NH, T]), ("kF", [QH, NH, T]), ("otok", [P, TB, D]), ("otok_pad", [P, D]), ("qaF", [P, 4, T]), ("kaF", [P, T]),
            ("kiF", [P, T]), ("va", [P, TB, HD]), ("wix", [P, TB, IDX_HEADS]), ("krt", [P, TB, ROPE]),
            ("kk", [P, TB, P]), ("score", [P, 1152]), ("bias", [P, 1280]), ("tab64", [P, 2, TB, HD]),
            ("tab32", [P, 2, TB, ROPE]), ("qtok", [P, TB, 4 * QH]), ("rtmp", [P, T]), ("lat", [P, TB, LATB * P]),
            ("vt", [P, TB, D // 2]), ("qst", [P, 2, T]), ("pT", [P, 2, T]), ("biasM", [P, T]), ("nmask", [P, P]),
            ("sm1", [P, 16]), ("m8", [P, 8]))
        (lhi, llo) = after_a("_l", ("lhi", [P, LATB, T], F32R), ("llo", [P, LATB, T], F32R))
        (xout,) = after_a("_x", ("xout", [P, TB, D]))
        pw = [sq[:, 0, :], sq[:, 1, :], ss[:], rinv[:]]

        vec_landed, x_landed = sem("vec_landed"), sem("x_landed")
        landed = [sem(f"landed{s}") for s in range(2)]
        ada_landed = [sem(f"ada_landed{s}") for s in range(2)]
        first_landed = [sem(f"first_landed{u}") for u in range(8)]
        tab_landed = sem("tab_landed")
        hi_split, lo_split = sem("hi_split"), sem("lo_split")
        tile_done = sem("tile_done")
        g_free = [sem(f"g_free{b}") for b in range(4)]
        aux_done = sem("aux_done")
        x_free = [sem(f"x_free{b}") for b in range(4)]
        gone = sem("gone")
        dve_step, act_step = sem("dve_step"), sem("act_step")
        vec_ready = sem("vec_ready")
        x_ready = sem("x_ready")
        sq_ready, ss_added, rt_ready = sem("sq_ready"), sem("ss_added"), sem("rt_ready")
        val_ready, val_hi = sem("val_ready"), sem("val_hi")
        act_ready = sem("act_ready")
        ada_acc, ada_used = sem("ada_acc"), sem("ada_used")
        dskip_ready = sem("dskip_ready")
        sg_ready, sg_used = sem("sg_ready"), sem("sg_used")
        c_ready = sem("c_ready")
        gf_ready, fx_ready = sem("gf_ready"), sem("fx_ready")
        gr_ready = sem("gr_ready")
        prep_a, prep_v = sem("prep_a"), sem("prep_v")
        acT_ready = sem("acT_ready")
        pre_ready, cv_ready, xf_ready = sem("pre_ready"), sem("cv_ready"), sem("xf_ready")
        xw_ready = sem("xw_ready")
        seg_ready, exp_ready, m_ready = sem("seg_ready"), sem("exp_ready"), sem("m_ready")
        st_ready, ytok_ready, yf_ready = sem("st_ready"), sem("ytok_ready"), sem("yf_ready")
        act_saved, bc_landed = sem("act_saved"), sem("bc_landed")
        k_ready, fm_ready = sem("k_ready"), sem("fm_ready")
        rl_ready, rl_used = sem("rl_ready"), sem("rl_used")
        lat_ready, lat_sum, lat_done = sem("lat_ready"), sem("lat_sum"), sem("lat_done")
        q_staged = [sem(f"q_staged{s}") for s in range(2)]
        lg_ready, p_ready, pT_ready, o_ready = sem("lg_ready"), sem("p_ready"), sem("pT_ready"), sem("o_ready")
        p_used = sem("p_used")
        o_copied, out_done = sem("o_copied"), sem("out_done")

        acum_dram = nc.dram_tensor("acum_dram", [HEADS, T], F32, kind="Internal").ap()

        def cols(w):
            return w.rearrange("(k p) n -> p k n", p=P)

        w_in, w_conv, w_o = cols(a["w_in"][0]), cols(a["w_conv_out"][0]), cols(a["w_o"][0])
        w_ssm = a["w_ssm_out"][0].rearrange("(g b p) n -> p g b n", p=P, b=2)
        w_up, w_down = cols(a["w_up"][0]), cols(a["w_down"][0])
        w_ada = cols(a["w_ada"][0])
        ffn = [[cols(a[f"w{j}_{n}_2"][0]) for n in ("gate", "up", "down")] for j in (1, 2)]
        w_in2, w_uq, w_ukv, w_out = (cols(a[n][0]) for n in ("w_in_2", "w_uq_2", "w_ukv_2", "w_out_2"))

        def unit(t, k=KB, n=UC):
            return t[:, 0:k * n].rearrange("p (k n) -> p k n", k=k)

        block = ctx.enter_context(nc.Block())

        @block.sync
        def _(sp):
            t = Tallies()
            slot = [0]
            started = [0]

            def load(*pieces, k=KB, n=UC):
                s = slot[0]
                slot[0] ^= 1
                if started[0] >= 2:
                    sp.wait_ge(lo_split, t["n"].now(-1))
                started[0] += 1
                at = 0
                for src in pieces:
                    w = src.shape[-1]
                    dst = unit(raw[s], k, n)[:, :, at:at + w]
                    sp.dma_start(dst, src).then_inc(landed[s], 16)
                    at += w
                t["n"].add()

            def load_ada(buf, dst, unit_no):
                sp.wait_ge(ada_used, t["ada"].now(-1))
                sp.dma_start(unit(dst), w_ada[:, :, bass.ds(unit_no * UC, UC)]).then_inc(ada_landed[buf], 16)
                t["ada"].add()

            def vec(dst, src):
                sp.dma_start(dst, src).then_inc(vec_landed, 16)

            def rows(v):
                return v.rearrange("(b p) -> b p", p=P)

            vec(v2[0:8, :], rows(a["ln1"][0]))
            vec(v2[8:16, :], rows(a["ln2"][0]))
            vec(v2[16:64, :], rows(a["b_ada"][0]))
            vec(v2[64:72, :], rows(a["c"][0]))
            vec(v2[72:104, :], rows(a["ssm_conv_b"][0]))
            for j in range(3):
                vec(v2[104 + 8 * j:112 + 8 * j, :], rows(a["conv_w"][0, j]))
            for j in range(4):
                vec(v1[32 * j:32 * j + 32, :], rows(a["ssm_conv_w"][0, j]))
            vec(ident[:], a["ident"])
            at = XB
            for name, n in (("ssm_norm_w", 16), ("final_norm", 8), ("g_ffn1_2", 8), ("g_mix_2", 8),
                            ("g_ffn2_2", 8), ("g_final_2", 8), ("g_q_lat_2", 3), ("g_kv_lat_2", 2)):
                v = a[name] if len(a[name].shape) == 1 else a[name][0]
                vec(v3[at:at + n, :], rows(v))
                at += n
            vec(dskip[:], a["d_skip"][0].rearrange("(b r) -> b r", r=2))
            vec(triu[:], a["triu"])
            vec(dtw[:, 0, :], a["dt_bias"].broadcast_to([P, HEADS]))
            vec(dtw[:, 1, :], a["a_log"].broadcast_to([P, HEADS]))
            for u in range(0, 8, 2):
                sp.dma_start(unit(araw[u]), w_ada[:, :, u * UC:(u + 1) * UC]).then_inc(first_landed[u], 16)
            t["ada"].add(8)

            def bc_load(g):
                if t["seg"].base + t["seg"].local:
                    sp.wait_ge(seg_ready, t["seg"].now())
                src = acum_dram[bass.ds(g * RH, RH), :].rearrange("r t -> (r t)").unsqueeze(0)
                sp.dma_start(bc[:].rearrange("p r t -> p (r t)"), src.broadcast_to([P, RH * T])).then_inc(bc_landed, 16)

            def scan_turn(g, gemm, ssd, outp):
                if gemm:
                    load(w_in[:, :, bass.ds(C_X + g * GW, GW)])
                if gemm and ssd and not outp:
                    sp.wait_ge(acT_ready, 1)
                    sp.dma_start(acum_dram, acT[0:HEADS, :]).then_inc(act_saved, 16)
                    sp.wait_ge(act_saved, 16)
                if ssd:
                    bc_load(g - 1)
                    t["seg"].add(RH)
                if gemm:
                    load(w_in[:, :, bass.ds(C_B + g * STATE, STATE)], w_in[:, :, bass.ds(C_C + g * STATE, STATE)])
                if outp:
                    sl = slot[0]
                    slot[0] ^= 1
                    sp.wait_ge(lo_split, t["n"].now(-1))
                    sp.dma_start(raw[sl][:, :].rearrange("p (o b n) -> p o b n", o=1, b=2),
                                 w_ssm[:, bass.ds(g - 2, 1), :, :]).then_inc(landed[sl], 16)
                    t["n"].add()
                if gemm:
                    load(w_in[:, :, bass.ds(C_Z + g * GW, GW)])

            load(w_in[:, :, C_DT:C_DT + HEADS], n=HEADS)
            scan_turn(0, True, False, False)
            scan_turn(1, True, True, False)
            with turns(sp, GROUPS - 2, t, {"n": 4, "seg": RH}) as i:
                scan_turn(i + 2, True, True, True)
            scan_turn(GROUPS, False, True, True)
            scan_turn(GROUPS + 1, False, False, True)

            with turns(sp, 2, t, {"n": 2, "ada": 2}) as i:
                for m in range(2):
                    load(w_in[:, :, bass.ds(C_GL + D + (2 * i + m) * UC, UC)])
                sp.wait_ge(tile_done, TILES_SCAN)
                for m in range(2):
                    load_ada(m, braw[m], 8 + 2 * i + m)
            with turns(sp, 4, t, {"n": 2, "ada": 2}) as i:
                load(w_in[:, :, bass.ds(C_CC + i * UC, UC)])
                load(w_in[:, :, bass.ds(C_CX + i * UC, UC)])
                for m in range(2):
                    load_ada(m, braw[m], 12 + 2 * i + m)
            with turns(sp, 2, t, {"n": 2, "ada": 2}) as i:
                for m in range(2):
                    load(w_in[:, :, bass.ds(C_CB + (2 * i + m) * UC, UC)])
                for m in range(2):
                    load_ada(m, braw[m], 20 + 2 * i + m)
            with turns(sp, 4, t, {"n": 2}) as i:
                load(w_in[:, :, bass.ds(C_GL + i * UC, UC)])
                load(w_conv[:, :, bass.ds(i * UC, UC)])
            with turns(sp, 2, t, {"n": 2}) as i:
                for m in range(2):
                    load(w_o[:, :, bass.ds((2 * i + m) * UC, UC)])
            with turns(sp, 4, t, {"n": 8}) as i:
                for j in range(4):
                    load(w_up[:, :, bass.ds(i * D + j * UC, UC)])
                for j in range(4):
                    load(w_down[:, bass.ds(i * KB, KB), j * UC:(j + 1) * UC])

            def swiglu(w):
                gate, up, down = w
                with turns(sp, 2, t, {"n": 12}) as i:
                    for j in range(4):
                        load(gate[:, :, bass.ds(i * D + j * UC, UC)])
                        load(up[:, :, bass.ds(i * D + j * UC, UC)])
                    for j in range(4):
                        load(down[:, bass.ds(i * KB, KB), j * UC:(j + 1) * UC])
                for j in range(3):
                    load(gate[:, :, 2 * D + j * UC:2 * D + (j + 1) * UC])
                    load(up[:, :, 2 * D + j * UC:2 * D + (j + 1) * UC])
                for j in range(4):
                    load(down[:, 16:22, j * UC:(j + 1) * UC], k=6)

            swiglu(ffn[0])
            load(w_in2[:, :, C_KA:C_QI], w_in2[:, :, C_KI:C_LAT], w_in2[:, :, C_KR:C_KR + ROPE])
            sp.wait_ge(tile_done, TILES_BEFORE_MIX2)
            sp.dma_start(tab64[:, 0], a["cos64"].rearrange("(b p) n -> p b n", p=P)).then_inc(tab_landed, 16)
            sp.dma_start(tab64[:, 1], a["sin64"].rearrange("(b p) n -> p b n", p=P)).then_inc(tab_landed, 16)
            sp.dma_start(tab32[:, 0], a["cos32"].rearrange("(b p) n -> p b n", p=P)).then_inc(tab_landed, 16)
            sp.dma_start(tab32[:, 1], a["sin32"].rearrange("(b p) n -> p b n", p=P)).then_inc(tab_landed, 16)
            sp.dma_start(nmask[:], a["nmask"]).then_inc(tab_landed, 16)
            for j in range(4):
                load(w_in2[:, :, C_QI + j * UC:C_QI + (j + 1) * UC])
            for j in range(2):
                load(w_in2[:, :, j * UC:(j + 1) * UC])
            for j in range(3):
                w = min(UC, C_KR - C_LAT - j * UC)
                load(w_in2[:, :, C_LAT + j * UC:C_LAT + j * UC + w])
            for j in range(2):
                load(w_uq[:, :, j * 4 * QH:(j + 1) * 4 * QH], k=3, n=4 * QH)
            for j in range(2):
                load(w_ukv[:, :, j * T:(j + 1) * T], k=2, n=T)
            for j in range(2):
                load(w_out[:, :, j * UC:(j + 1) * UC])
            sp.wait_ge(fm_ready, FM_ALL)
            sp.dma_start(qst[:, 0, :].unsqueeze(1), qaF[:, 0:1, :]).then_inc(q_staged[0], 16)
            with turns(sp, NH // 2 - 1, t, {"q": 2 * TB}) as i:
                t["q"].add(2 * TB)
                sp.wait_ge(lg_ready, t["q"].now())
                sp.dma_start(qst[:, 0, :].unsqueeze(1), qaF[:, bass.ds(i + 1, 1), :]).then_inc(q_staged[0], 16)
            t["q"].add(2 * TB)
            sp.wait_ge(lg_ready, t["q"].now())
            with turns(sp, NH // 2, t, {"q": 2 * TB}) as i:
                for s in range(2):
                    sp.wait_ge(lg_ready, t["q"].now(TB * (s - 1)))
                    sp.dma_start(qst[0:QH, s, :].unsqueeze(1), qF[:, bass.ds(2 * i + s, 1), :])\
                        .then_inc(q_staged[s], 16)
                t["q"].add(2 * TB)
            for j in range(2, 4):
                load(w_out[:, :, j * UC:(j + 1) * UC])
            swiglu(ffn[1])
            for b in range(TB):
                sp.wait_ge(o_copied, 2 * (b + 1))
                sp.dma_start(out[0, b * P:(b + 1) * P, :], xout[:, b, :]).then_inc(out_done, 16)
            sp.wait_ge(out_done, 16 * TB)

        @block.tensor
        def _(pe):
            t = Tallies()
            slot = [0]

            def next_unit():
                s = slot[0]
                slot[0] ^= 1
                t["n"].add()
                pe.wait_ge(lo_split, t["n"].now())
                return s

            def take_g(b):
                used = t[f"g{b}"]
                if used.i is not None or used.now() != 0:
                    pe.wait_ge(g_free[b], used.now())
                used.add()
                return G[b]

            def take_x(b):
                used = t[f"x{b}"]
                if used.i is not None or used.now() != 0:
                    pe.wait_ge(x_free[b], used.now())
                used.add()
                return X[b]

            def fm_tile(s, m, rh, rl, k=KB, n=UC, b=None, each=None):
                bank = take_g(2 * s + m if b is None else b)
                wh, wl = unit(whi[s], k, n), unit(wlo[s], k, n)
                f = slice(m * P, (m + 1) * P)
                for j in range(k):
                    if each is not None:
                        pe.wait_ge(act_ready, each.now(j + 1))
                    pe.matmul(bank[:], wh[:, j, f], rh[:, j, :], start=(j == 0), stop=False)
                    pe.matmul(bank[:], wh[:, j, f], rl[:, j, :], start=False, stop=False)
                    last = pe.matmul(bank[:], wl[:, j, f], rh[:, j, :], start=False, stop=(j == k - 1))
                last.then_inc(tile_done, 1)

            def fm_unit(rh, rl, k=KB, each=None):
                s = next_unit()
                for m in range(2):
                    fm_tile(s, m, rh, rl, k, each=each if m == 0 else None)

            def tok_part(dst, s, b, k, n, rh, rl, width=None, each=None):
                wh, wl = unit(whi[s], k, width or n), unit(wlo[s], k, width or n)
                tk = slice(b * P, (b + 1) * P)
                for j in range(k):
                    if each is not None:
                        pe.wait_ge(act_ready, each.now(j + 1))
                    pe.matmul(dst, rh[:, j, tk], wh[:, j, 0:n], start=(j == 0), stop=False)
                    pe.matmul(dst, rl[:, j, tk], wh[:, j, 0:n], start=False, stop=False)
                    last = pe.matmul(dst, rh[:, j, tk], wl[:, j, 0:n], start=False, stop=(j == k - 1))
                return last

            def tok_unit(n=UC, each=None):
                s = next_unit()
                for half in range(2):
                    bank = take_g(2 * s + half)
                    for b in range(2):
                        last = tok_part(bank[:, b * UC:b * UC + n], s, 2 * half + b, KB, n, ahi, alo, UC,
                                        each if half + b == 0 else None)
                    last.then_inc(tile_done, 1)

            def column_sum():
                t["ss"].add(KB - 1)
                bank = take_x(1)
                pe.wait_ge(ss_added, t["ss"].now())
                pe.matmul(bank[:], ones[:], ss[:], start=True, stop=True).then_inc(aux_done, 1)

            def operand(n):
                t["op"].add(n)
                pe.wait_ge(act_ready, t["op"].now())

            pe.wait_ge(dskip_ready, 1)
            pe.wait_ge(vec_landed, 16 * VECS)
            bank = take_x(0)
            pe.transpose(bank[:, 0:P], v1[:], ident[:])
            pe.transpose(bank[:, P:2 * P], v2[:], ident[:])
            pe.transpose(bank[:, 2 * P:2 * P + VROWS], v3[0:VROWS, :], ident[0:VROWS, 0:VROWS]).then_inc(aux_done, 1)
            pe.wait_ge(x_landed, 16)
            for k in range(KB):
                bank = take_g(k % 4)
                for b in range(TB):
                    last = pe.transpose(bank[:, b * P:(b + 1) * P], xin[:, b, k * P:(k + 1) * P], ident[:])
                last.then_inc(tile_done, 1)

            def ada_columns(at, acc=badacc):
                b = t["ada"].local % 2
                t["ada"].add()
                pe.wait_ge(ada_acc, t["ada"].now())
                for m in range(2):
                    last = pe.matmul(X[3][:, bass.ds(at + m, 1)], acc[:, b, m * P:(m + 1) * P],
                                     ones[:, 0:1], start=True, stop=True)
                last.then_inc(ada_used, 1)

            pe.wait_ge(gone, 1)
            column_sum()
            take_x(3)
            pe.wait_ge(c_ready, 1)
            for u in range(8):
                if u not in FIRST_ON_PE:
                    ada_columns(2 * u, adacc)
                    continue
                pe.wait_ge(first_landed[u], 16)
                w = unit(araw[u])
                for m in range(2):
                    for k in range(KB):
                        last = pe.matmul(X[3][:, 2 * u + m:2 * u + m + 1], w[:, k, m * P:(m + 1) * P], cact[:, k:k + 1],
                                         start=(k == 0), stop=(k == KB - 1))
                last.then_inc(ada_used, 1)

            s = next_unit()
            bank = take_g(2 * s)
            for b in range(TB):
                last = tok_part(bank[:, b * HEADS:(b + 1) * HEADS], s, b, KB, HEADS, ahi, alo,
                                each=t["op"] if b == 0 else None)
            last.then_inc(tile_done, 1)
            t["op"].add(KB)

            def scan_turn(gemm, ssd, outp):
                if gemm:
                    sx = next_unit()
                    fm_tile(sx, 0, ahi, alo)
                if outp:
                    t["ss"].add(1)
                    bank = take_x(2)
                    pe.wait_ge(ss_added, t["ss"].now())
                    pe.matmul(bank[:], ones[:], ss[:], start=True, stop=True).then_inc(aux_done, 1)
                if gemm:
                    fm_tile(sx, 1, ahi, alo)
                if ssd:
                    t["xf"].add(4)
                    pe.wait_ge(xf_ready, t["xf"].now())
                    for half in range(2):
                        bank = take_x(half)
                        for c in range(2):
                            ck = slice((2 * half + c) * P, (2 * half + c + 1) * P)
                            for b in range(2):
                                last = pe.transpose(bank[:, c * GW + b * P:c * GW + (b + 1) * P], xf[:, b, ck], ident[:])
                        last.then_inc(aux_done, 1)
                    bank = take_x(2)
                    for c in range(TB):
                        last = pe.transpose(bank[:, c * P:(c + 1) * P], xf[:, 2, c * P:(c + 1) * P], ident[:])
                    last.then_inc(aux_done, 1)
                    bank = take_x(3)
                    for c in range(TB):
                        ck = slice(c * P, (c + 1) * P)
                        last = pe.matmul(bank[:, ck], xf[:, 2, ck], xf[:, 3, ck], start=True, stop=True)
                    last.then_inc(aux_done, 1)
                if gemm:
                    fm_unit(ahi, alo)
                if outp:
                    s = next_unit()
                    operand(2)
                    for m in range(KB):
                        fm_tile(s, m, yhi, ylo, k=2, n=D, b=(2 * s + m) % 4)
                if ssd:
                    y0, y1 = take_x(0), take_x(1)
                    for r in range(RH):
                        t["m"].add()
                        pe.wait_ge(m_ready, t["m"].now())
                        for c in range(TB):
                            bank = (y0, y1)[c // 2]
                            at = (c % 2) * GW + r * HEAD_DIM
                            last = pe.matmul(bank[:, at:at + HEAD_DIM], seg[:, r, c * P:(c + 1) * P],
                                             xdt[:, c, r * HEAD_DIM:(r + 1) * HEAD_DIM], start=True, stop=True)
                    last.then_inc(aux_done, 1)
                    bank, bank3 = take_x(2), take_x(3)
                    t["xw"].add()
                    pe.wait_ge(xw_ready, t["xw"].now())
                    for c in range(3):
                        dst = bank3[:, 0:GW] if c == 2 else bank[:, c * GW:(c + 1) * GW]
                        last = pe.matmul(dst, btok[:, c, :], xw[:, c, :], start=True, stop=True)
                    last.then_inc(aux_done, 1)
                if gemm:
                    sz = next_unit()
                    fm_tile(sz, 0, ahi, alo)
                if ssd:
                    bank, bank3 = take_x(2), take_x(3)
                    t["st"].add()
                    pe.wait_ge(st_ready, t["st"].now())
                    for c in range(1, TB):
                        dst = bank3[:, 0:GW] if c == 3 else bank[:, (c - 1) * GW:c * GW]
                        last = pe.matmul(dst, xf[:, 3, c * P:(c + 1) * P], states[:, c - 1, :], start=True, stop=True)
                    last.then_inc(aux_done, 1)
                if gemm:
                    fm_tile(sz, 1, ahi, alo)
                if ssd:
                    t["yt"].add()
                    pe.wait_ge(ytok_ready, t["yt"].now())
                    for b in range(2):
                        bank = take_x(b)
                        for c in range(TB):
                            last = pe.transpose(bank[:, c * P:(c + 1) * P], ytok[:, c, b * P:(b + 1) * P], ident[:])
                        last.then_inc(aux_done, 1)

            scan_turn(True, False, False)
            bank, bank1, bank2 = take_x(0), take_x(1), take_x(2)
            pe.wait_ge(prep_v, 3)
            decays = dts[:, TMP, :, :]
            pe.matmul(bank[:, 0:P], triu[:], decays, start=True, stop=True).then_inc(aux_done, 1)
            pe.matmul(bank1[:, 0:P], ones[:], decays, start=True, stop=True).then_inc(aux_done, 1)
            for c in range(TB):
                last = pe.matmul(bank2[0:HEADS, c * P:(c + 1) * P], dts[:, TMP, c, :], triu[:], start=True, stop=True)
            last.then_inc(aux_done, 1)
            scan_turn(True, True, False)
            with turns(pe, GROUPS - 2, t, {"n": 4, "g0": 4, "g1": 4, "g2": 3, "g3": 3, "x0": 3, "x1": 3, "x2": 4,
                                           "x3": 3, "ss": 1, "op": 2, "xf": 4, "m": 4, "xw": 1, "st": 1, "yt": 1}
                       ):
                scan_turn(True, True, True)
            scan_turn(False, True, True)
            scan_turn(False, False, True)

            take_x(3)
            both = {"n": 2, "g0": 1, "g1": 1, "g2": 1, "g3": 1}
            with turns(pe, 2, t, {**both, "ada": 2}) as i:
                for m in range(2):
                    fm_unit(ahi, alo)
                    ada_columns(16 + 4 * i + 2 * m)
            with turns(pe, 4, t, {**both, "ada": 2}) as i:
                for m in range(2):
                    fm_unit(ahi, alo)
                    ada_columns(24 + 4 * i + 2 * m)
            with turns(pe, 2, t, {**both, "ada": 2}) as i:
                for m in range(2):
                    fm_unit(ahi, alo)
                    ada_columns(40 + 4 * i + 2 * m)
            operand(KB)
            with turns(pe, 4, t, both):
                fm_unit(ahi, alo)
                fm_unit(bhi, blo)
            operand(KB)
            with turns(pe, 2, t, both):
                for m in range(2):
                    fm_unit(chi, clo)

            def slab(ups, k, each=None):
                for j in range(ups):
                    fm_unit(ahi, alo, each=each if j == 0 else None)
                for j in range(4):
                    fm_unit(hhi, hlo, k, each=t["op"] if j == 0 else None)
                t["op"].add(k)

            column_sum()
            normed = Tally("normed")
            normed.base = t["op"].now()
            t["op"].add(KB)
            with turns(pe, 4, t, {"n": 8, "g0": 4, "g1": 4, "g2": 4, "g3": 4, "op": KB}):
                slab(4, KB, normed)

            def swiglu(twice=False):
                fm_unit(ahi, alo, each=t["op"])
                t["op"].add(KB)
                s = next_unit()
                fm_tile(s, 0, ahi, alo)
                t["ss"].add(KB - 1)
                bank, bank2 = take_x(1), take_x(0) if twice else None
                pe.wait_ge(ss_added, t["ss"].now())
                pe.matmul(bank[:], ones[:], ss[:], start=True, stop=True).then_inc(aux_done, 1)
                if twice:
                    pe.matmul(bank2[:], ones[:], rr[:], start=True, stop=True).then_inc(aux_done, 1)
                fm_tile(s, 1, ahi, alo)
                slab(6, KB)
                slab(8, KB)
                slab(6, 6)

            swiglu(twice=True)

            column_sum()
            tok_unit(M_W, t["op"])
            t["op"].add(KB)
            t["k"].add(2)
            pe.wait_ge(k_ready, t["k"].now())
            kview = qtok[:, :, 0:P]
            for b2, src in ((0, kk), (1, kview)):
                bank = take_x(b2)
                for b in range(TB):
                    last = pe.transpose(bank[:, b * P:(b + 1) * P], src[:, b, :], ident[:])
                last.then_inc(aux_done, 1)

            def turn_heads(pairs=True):
                t["k"].add()
                pe.wait_ge(k_ready, t["k"].now())
                for j in range(2 if pairs else 4):
                    bank = take_x(j % 2)
                    w = P if pairs else QH
                    for b in range(TB):
                        last = pe.transpose(bank[0:w, b * P:(b + 1) * P], qtok[:, b, j * w:(j + 1) * w], ident[:])
                    last.then_inc(aux_done, 1)

            def index_scores():
                t["fm"].add(2)
                pe.wait_ge(fm_ready, t["fm"].now())
                for j in range(2):
                    for h in range(2):
                        rows = slice(h * HD, (h + 1) * HD)
                        for q in range(1, TB):
                            bank = take_x(2 + t["rot"].local % 2)
                            t["rot"].add()
                            w = (q + 1) * P
                            pe.matmul(bank[:, 0:w], qst[rows, j, q * P:(q + 1) * P], kiF[rows, 0:w],
                                      start=True, stop=True).then_inc(aux_done, 1)

            t["fm"].add(2)
            for u in range(4):
                tok_unit()
                if u:
                    index_scores()
                turn_heads()
            for u in range(2):
                tok_unit()
                if u == 0:
                    index_scores()
                turn_heads()
            for u in range(3):
                tok_unit(min(UC, LATB * P - u * UC))
            pe.wait_ge(lat_done, 1)
            for j in range(LATB):
                bank = take_x(j % 2)
                for b in range(TB):
                    last = pe.transpose(bank[:, b * P:(b + 1) * P], lat[:, b, j * P:(j + 1) * P], ident[:])
                last.then_inc(aux_done, 1)
            operand(LATB)

            def latent_unit(first, k, n):
                s = next_unit()
                for b in range(TB):
                    bank = take_g(2 * s + b % 2)
                    tok_part(bank[:, 0:n], s, b, k, n, lhi[:, first:first + k, :], llo[:, first:first + k, :])\
                        .then_inc(tile_done, 1)

            for u in range(2):
                latent_unit(0, 3, 4 * QH)
                turn_heads(False)
            for u in range(2):
                latent_unit(3, 2, T)
                turn_heads(False)

            t["rot"].base, t["rot"].local = 0, 0
            for latent in range(2):
                with turns(pe, NH // 2, t, {"qs0": 16, "qs1": 16 * latent, "x0": 4, "x1": 4, "x2": 8, "x3": 8, "p": 8}) as i:
                    items = [(h, q) for h in range(2) for q in range(TB)]

                    def logits(n):
                        h, q = items[n]
                        if q == 0 and (latent or h == 0):
                            t[f"qs{h}"].add(16)
                            pe.wait_ge(q_staged[h], t[f"qs{h}"].now())
                        w = (q + 1) * P
                        bank = take_x(n % 2)
                        if latent:
                            lhs, rhs = qst[0:QH, h, q * P:(q + 1) * P], kF[:, bass.ds(2 * i + h, 1), 0:w]
                        else:
                            rows = slice(h * HD, (h + 1) * HD)
                            lhs, rhs = qst[rows, 0, q * P:(q + 1) * P], kaF[rows, 0:w]
                        pe.matmul(bank[:, 0:w], lhs, rhs, start=True, stop=True).then_inc(aux_done, 1)

                    def turn_p(n):
                        h, q = items[n]
                        t["p"].add()
                        bank = take_x(2)
                        pe.wait_ge(p_ready, t["p"].now())
                        for j in range(q + 1):
                            last = pe.transpose(bank[:, j * P:(j + 1) * P], pw[n % 4][:, j * P:(j + 1) * P], ident[:])
                        last.then_inc(aux_done, 1)

                    def values(n):
                        h, q = items[n]
                        bank = take_x(3)
                        pe.wait_ge(pT_ready, t["p"].now(0 if n == len(items) - 1 else -1))
                        for j in range(q + 1):
                            v = vt[:, j, bass.ds((2 * i + h) * HD, HD)] if latent else va[:, j, :]
                            last = pe.matmul(bank[:, 0:HD], pT[:, n % 2, j * P:(j + 1) * P], v,
                                             start=(j == 0), stop=(j == q))
                        last.then_inc(aux_done, 1)

                    for n in range(len(items) + 3):
                        if n < len(items):
                            logits(n)
                        if 2 <= n < len(items) + 2:
                            turn_p(n - 2)
                        if n >= 3:
                            values(n - 3)
            pe.wait_ge(o_ready, 1)
            for k in range(KB):
                bank = take_x(k % 4)
                for b in range(TB):
                    last = pe.transpose(bank[:, b * P:(b + 1) * P], otok[:, b, k * P:(k + 1) * P], ident[:])
                last.then_inc(aux_done, 1)
            operand(KB)
            for u in range(4):
                fm_unit(ahi, alo)
            swiglu()
            column_sum()
            pe.wait_ge(x_ready, XREADY_END)
            for b in range(TB):
                for half in range(2):
                    bank = take_x(2 * (b % 2) + half)
                    for j in range(4):
                        last = pe.transpose(bank[:, j * P:(j + 1) * P], xT[:, 4 * half + j, b * P:(b + 1) * P], ident[:])
                    last.then_inc(aux_done, 1)

        @block.scalar
        def _(act):
            t = Tallies()
            slot = [0]

            def split_next(loads=1):
                s = slot[0]
                slot[0] ^= 1
                t[f"land{s}"].add(16 * loads)
                act.wait_ge(landed[s], t[f"land{s}"].now())
                if s or t["tile"].i is not None or t["tile"].now():
                    act.wait_ge(tile_done, t["tile"].now())
                act.activation(whi[s][:], raw[s][:], ACT.Copy).then_inc(hi_split, 1)

            def tile():
                t["tile"].add()
                act.wait_ge(tile_done, t["tile"].now())

            def aux():
                t["aux"].add()
                act.wait_ge(aux_done, t["aux"].now())

            def link(ins):
                t["step"].add()
                ins.then_inc(act_step, 1)
                act.wait_ge(act_step, t["step"].now())

            def squares():
                for k in range(KB):
                    t["x"].add()
                    act.wait_ge(x_ready, t["x"].now())
                    if k >= 2:
                        act.wait_ge(ss_added, t["ss"].now(max(1, k - 2)))
                    act.activation(sq[:, k % 2, :], xT[:, k, :], ACT.Square).then_inc(sq_ready, 1)
                t["ss"].add(KB - 1)

            def root(bank, b, width):
                act.activation(warm[:], epsT[:], ACT.Sqrt)
                aux()
                act.activation(rinv[:], bank[:], ACT.Sqrt, bias=epsT[:], scale=1.0 / width).then_inc(rt_ready, 1)

            def high(dst, src, bias=None):
                t["val"].add()
                act.wait_ge(val_ready, t["val"].now())
                if bias is None:
                    act.activation(dst, src, ACT.Copy).then_inc(val_hi, 1)
                else:
                    act.activation(dst, src, ACT.Identity, bias=bias).then_inc(val_hi, 1)

            def norm(hi=None, lo_bias=None):
                squares()
                root(X[1], 1, D)
                if hi is not None:
                    for k in range(KB):
                        high(hi[:, k, :], sq[:, k % 2, :], None if lo_bias is None else lo_bias[:, k:k + 1])

            act.dma_start(xin[:], a["x"][0].rearrange("(b p) n -> p b n", p=P)).then_inc(x_landed, 16)
            for u in range(1, 8, 2):
                act.dma_start(araw[u][:, :].rearrange("p (k n) -> p k n", k=KB), w_ada[:, :, u * UC:(u + 1) * UC])\
                    .then_inc(first_landed[u], 16)
            act.wait_ge(vec_ready, 1)
            act.activation(cact[:], cT, ACT.Silu).then_inc(c_ready, 1)
            act.wait_ge(gone, 2)
            t["aux"].add()
            t["tile"].add(KB)
            squares()
            root(X[1], 1, D)
            t["land0"].add(16)
            act.wait_ge(landed[0], 16)
            slot[0] = 1
            act.activation(whi[0][:, 0:KB * HEADS], raw[0][:, 0:KB * HEADS], ACT.Copy).then_inc(hi_split, 1)
            for k in range(KB):
                high(ahi[:, k, :], sq[:, k % 2, :], modT[:, 0, k:k + 1])

            split_next()
            t["tile"].add()
            act.wait_ge(prep_v, 1)
            z, e, w = dts[:, TMP], dts[:, DT], dts[:, AC]
            link(act.activation(e, z, ACT.Abs))
            link(act.activation(e, e, ACT.Exp, scale=-1.0))
            act.activation(dtw[:, 1, :], dtw[:, 1, :], ACT.Exp).then_inc(prep_a, 1)
            act.wait_ge(prep_v, 2)
            act.activation(dts[:, EAC], w, ACT.Ln).then_inc(prep_a, 1)

            def unit(loads=1):
                s = slot[0] ^ 1
                split_next(loads)
                return s

            def conv_in(b, m, blk):
                tile()
                act.activation(cv[:, m, :], G[b][:], ACT.Identity, scale=v1T[:, 3, bass.ds(blk, 1)],
                               bias=v2T[:, bass.ds(convb0 + blk, 1)])
                act.activation(pre[:, m, 3:3 + T], G[b][:], ACT.Copy).then_inc(pre_ready, 1)

            def scan_turn(g, gemm, ssd, outp):
                if gemm:
                    s = unit(2)
                    if t["xf"].i is not None or t["xf"].now():
                        act.wait_ge(xf_ready, t["xf"].now())
                    conv_in(2 * s, 0, 2 * g)
                if outp:
                    root(X[2], 2, GW)
                if gemm:
                    conv_in(2 * s + 1, 1, 2 * g + 1)
                if outp:
                    for b in range(2):
                        high(yhi[:, b, :], sq[:, b, :])
                if gemm:
                    s = unit()
                if ssd:
                    t["aux"].add(2)
                    aux()
                    act.activation(btok[:], X[2][:].rearrange("p (c n) -> p c n", c=TB), ACT.Copy)\
                        .then_inc(x_free[2], 1)
                    t["aux"].add(1)
                    t["bc"].add(16)
                    act.wait_ge(bc_landed, t["bc"].now())
                    for r in range(RH):
                        for c in range(TB):
                            last = act.activation(seg[:, r, c * P:(c + 1) * P], bc[:, r, c * P:(c + 1) * P], ACT.Relu,
                                                  bias=dts[:, AC, c, bass.ds((g - 1) * RH + r, 1)], scale=-1.0)
                        last.then_inc(seg_ready, 1)
                    for r in range(RH):
                        t["seg"].add()
                        act.wait_ge(seg_ready, t["seg"].now())
                        act.activation(seg[:, r, :], seg[:, r, :], ACT.Exp, scale=-1.0).then_inc(exp_ready, 1)
                if gemm:
                    for m in range(2):
                        conv_in(2 * s + m, 2 + m, XB + GROUPS * m + g)
                if outp:
                    unit()
                    t["tile"].add(KB)
                if gemm:
                    s = unit()
                if ssd:
                    t["aux"].add(1 + 1 + 1 + 2)
                    for b in range(2):
                        t["yf"].add()
                        act.wait_ge(yf_ready, t["yf"].now())
                        act.activation(sq[:, b, :], yf[:, b, :], ACT.Square).then_inc(sq_ready, 1)
                if gemm:
                    for m in range(2):
                        tile()
                        act.activation(zs[:, m, :], G[2 * s + m][:], ACT.Silu).then_inc(g_free[2 * s + m], 1)
                    for b in range(4):
                        t["cv"].add()
                        act.wait_ge(cv_ready, t["cv"].now())
                        act.activation(xf[:, b, :], cv[:, b, :], ACT.Silu).then_inc(xf_ready, 1)
                    t["xf"].add(4)

            scan_turn(0, True, False, False)
            t["aux"].add(2)
            aux()
            act.activation(acT[0:HEADS, :], X[2][0:HEADS, :], ACT.Copy).then_inc(acT_ready, 1)
            act.wait_ge(prep_v, 4)
            act.activation(dts[:, EAC], X[0][:, 0:P].rearrange("p (c h) -> p c h", c=TB), ACT.Exp)
            act.activation(dts[:, EEND], X[1][:, 0:P].rearrange("p (c h) -> p c h", c=TB), ACT.Exp)
            act.activation(dts[:, TOEND], dts[:, TOEND], ACT.Exp).then_inc(prep_a, 1)
            scan_turn(1, True, True, False)
            with turns(act, GROUPS - 2, t, {"land0": 48, "land1": 32, "tile": 14, "aux": 10, "ss": 0, "val": 2,
                                            "xf": 4, "seg": 4, "bc": 16, "yf": 2, "cv": 4}) as i:
                scan_turn(i + 2, True, True, True)
            scan_turn(GROUPS, False, True, True)
            scan_turn(GROUPS + 1, False, False, True)
            t["ss"].add(GROUPS)

            def gated(dst, s, m, func, used=False):
                tile()
                if used and m == 0:
                    act.wait_ge(sg_used, t["sg"].now())
                if used:
                    t["sg"].add()
                act.activation(dst, G[2 * s + m][:], func).then_inc(sg_ready, 1)

            both = {"land0": 16, "land1": 16}
            t["sg"].add(1)
            with turns(act, 2, t, {**both, "tile": 4, "sg": 4}):
                for u in range(2):
                    s = unit()
                    for m in range(2):
                        gated(sq[:, m, :], s, m, ACT.Sigmoid, used=True)
            with turns(act, 4, t, {**both, "tile": 4, "sg": 2}):
                s = unit()
                for m in range(2):
                    gated(ccs[:, m, :], s, m, ACT.Copy, used=True)
                unit()
                t["tile"].add(2)
            with turns(act, 2, t, {**both, "tile": 4, "val": 4}) as i:
                for u in range(2):
                    unit()
                    for m in range(2):
                        high(bhi[:, bass.ds(4 * i + 2 * u + m, 1), :], sq[:, m, :].unsqueeze(1))
                    t["tile"].add(2)
            with turns(act, 4, t, {**both, "tile": 4, "val": 2}) as i:
                s = unit()
                for m in range(2):
                    gated(ccs[:, m, :], s, m, ACT.Sigmoid)
                unit()
                for m in range(2):
                    high(chi[:, bass.ds(2 * i + m, 1), :], sq[:, m, :].unsqueeze(1))
                t["tile"].add(2)
            with turns(act, 2, t, {**both, "tile": 4}):
                for u in range(2):
                    unit()
                    t["tile"].add(2)
            norm(ahi, modT[:, 3, :])
            with turns(act, 4, t, {"land0": 64, "land1": 64, "tile": 16, "val": 8}):
                for u in range(4):
                    s = unit()
                    for m in range(2):
                        gated(gs[:, m, :], s, m, ACT.Relu)
                        high(hhi[:, 2 * u + m, :], sq[:, m, :])
                for u in range(4):
                    unit()
                    t["tile"].add(2)

            def swiglu(gain, loads_after=1, last=False, twice=False):
                act.wait_ge(tile_done, t["tile"].now())
                for k in range(KB):
                    t["x"].add()
                    act.wait_ge(x_ready, t["x"].now())
                    if twice and k == 0:
                        act.wait_ge(gf_ready, 1)
                    act.activation(ahi[:, k, :], xT[:, k, :], ACT.Identity, scale=gain[:, k:k + 1]).then_inc(val_hi, 1)
                unit()
                for k in range(KB):
                    if k >= 2:
                        act.wait_ge(ss_added, t["ss"].now(max(1, k - 2)))
                    if twice:
                        act.activation(gs[:, k % 2, :], xT[:, k, :], ACT.Square, scale=finalT[:, k:k + 1])
                    act.activation(sq[:, k % 2, :], xT[:, k, :], ACT.Square).then_inc(sq_ready, 1)
                t["ss"].add(KB - 1)
                t["tile"].add(2)
                unit()
                root(X[1], 1, D)
                if twice:
                    t["aux"].add()
                    t["x"].add(KB)
                    act.wait_ge(fx_ready, 1)
                    act.activation(rr[:], rr[:], ACT.Sqrt, bias=epsT[:]).then_inc(rt_ready, 1)

                def slab(pairs, loads_after=1, last=False, first=False):
                    for u in range(pairs):
                        if u or not first:
                            unit()
                        for m in range(2):
                            t["gr"].add()
                            act.wait_ge(gr_ready, t["gr"].now())
                            act.activation(gs[:, m, :], gs[:, m, :], ACT.Silu).then_inc(sg_ready, 1)
                        if u or not first:
                            t["tile"].add(2)
                            unit()
                        for m in range(2):
                            high(hhi[:, 2 * u + m, :], sq[:, m, :])
                        t["tile"].add(2)
                    for u in range(4):
                        if not (last and u == 3):
                            unit(loads_after if u == 3 else 1)
                        t["tile"].add(2)

                slab(4, first=True)
                slab(4)
                slab(3, loads_after, last)
                t["x"].add(2 * KB)

            t["x"].add(3 * KB)
            swiglu(gf, loads_after=3, twice=True)

            norm(ahi)

            def fm(dst, b, w=P):
                aux()
                t["fm"].add()
                act.activation(dst, X[b][0:w, :], ACT.Copy).then_inc(fm_ready, 1)
                act.wait_ge(fm_ready, t["fm"].now())
                act.sem_inc(x_free[b], 1)

            unit()
            t["tile"].add(2)
            fm(kaF[:], 0)
            fm(kiF[:], 1)

            def index_relus():
                for n in range(12):
                    aux()
                    q = n % 3 + 1
                    w = (q + 1) * P
                    if t["rl"].local >= 2:
                        act.wait_ge(rl_used, t["rl"].now(-1))
                    t["rl"].add()
                    act.activation(pT[:, n % 2, 0:w], X[2 + n % 2][:, 0:w], ACT.Relu).then_inc(rl_ready, 1)

            for u in range(4):
                unit()
                t["tile"].add(2)
                if u:
                    index_relus()
                for j in range(2):
                    fm(qst[:, j, :], j)
            for u in range(2):
                unit()
                t["tile"].add(2)
                if u == 0:
                    index_relus()
                for j in range(2):
                    fm(qaF[:, 2 * u + j, :], j)
            for u in range(3):
                s = unit()
                w = min(UC, LATB * P - u * UC)
                for half in range(2):
                    tile()
                    link(act.activation(lat[:, 2 * half:2 * half + 2, u * UC:u * UC + w],
                                        G[2 * s + half][:].rearrange("p (b n) -> p b n", b=2)[:, :, 0:w], ACT.Copy))
                    act.sem_inc(g_free[2 * s + half], 1)
            for b in range(TB):
                link(act.activation(sq[:, 0, 0:384], lat[:, b, 0:384], ACT.Square, accum_out=sm1[:, b:b + 1]))
                link(act.activation(sq[:, 0, 0:256], lat[:, b, 384:640], ACT.Square, accum_out=sm1[:, 4 + b:5 + b]))
            link(act.activation(sm1[:, 0:4], sm1[:, 0:4], ACT.Sqrt, bias=epsT[:], scale=1.0 / 384))
            act.activation(sm1[:, 4:8], sm1[:, 4:8], ACT.Sqrt, bias=epsT[:], scale=1.0 / 256).then_inc(lat_ready, 1)
            for j in range(LATB):
                aux()
                act.activation(lhi[:, j, :], X[j % 2][:], ACT.Identity, scale=v3T[:, latg0 + j:latg0 + j + 1])\
                    .then_inc(val_hi, 1)
            for u in range(2):
                unit()
                t["tile"].add(4)
                for j in range(4):
                    fm(qF[:, 4 * u + j, :], j % 2, QH)
            for u in range(2):
                unit()
                t["tile"].add(4)
                for j in range(4):
                    fm(kF[:, 4 * u + j, :], j % 2, QH)
            for latent in range(2):
                with turns(act, NH // 2, t, {"aux": 24, "lg": 8, "pT": 8}):
                    for n in range(11):
                        if n < 8:
                            w = (n % TB + 1) * P
                            t["lg"].add()
                            t["aux"].add()
                            act.wait_ge(lg_ready, t["lg"].now())
                            act.activation(pw[n % 4][:, 0:w], pw[n % 4][:, 0:w], ACT.Exp, bias=sm1[:, n % 4:n % 4 + 1],
                                           accum_out=sm1[:, 8 + n % 4:9 + n % 4]).then_inc(p_ready, 1)
                        if 2 <= n < 10:
                            w = ((n - 2) % TB + 1) * P
                            aux()
                            t["pT"].add()
                            act.activation(pT[:, n % 2, 0:w], X[2][:, 0:w], ACT.Copy).then_inc(pT_ready, 1)
                            act.wait_ge(pT_ready, t["pT"].now())
                            act.sem_inc(x_free[2], 1)
                        if n >= 3:
                            t["aux"].add()
            for k in range(KB):
                aux()
                act.activation(ahi[:, k, :], X[k % 4][:], ACT.Copy).then_inc(val_hi, 1)
            for u in range(4):
                unit()
                t["tile"].add(2)
            swiglu(gf2T, last=True)
            norm()

        @block.gpsimd
        def _(pool):
            pool.memset(ones[:], 1.0).then_inc(gone, 1)
            pool.memset(epsT[:], EPS).then_inc(gone, 1)

        @block.vector
        def _(dve):
            t = Tallies()
            slot = [0]
            tt, ts, stt = dve.tensor_tensor, dve.tensor_scalar, dve.scalar_tensor_tensor

            def unit(last=False):
                s = slot[0]
                if not last:
                    slot[0] ^= 1
                    t["hi"].add()
                    dve.wait_ge(hi_split, t["hi"].now())
                    tt(wlo[s][:], raw[s][:], r32(whi[s][:]), ALU.subtract).then_inc(lo_split, 1)
                return s ^ 1

            def tile():
                t["tile"].add()
                dve.wait_ge(tile_done, t["tile"].now())

            def aux():
                t["aux"].add()
                dve.wait_ge(aux_done, t["aux"].now())

            def link(ins):
                t["step"].add()
                ins.then_inc(dve_step, 1)
                dve.wait_ge(dve_step, t["step"].now())

            def signal(ins, s, name, free=None):
                t[name].add()
                ins.then_inc(s, 1)
                if free is not None:
                    dve.wait_ge(s, t[name].now())
                    dve.sem_inc(free, 1)

            def low(dst, hi, src, bias=None):
                t["vhi"].add()
                t["op"].add()
                dve.wait_ge(val_hi, t["vhi"].now())
                if bias is None:
                    tt(dst, src, r32(hi), ALU.subtract).then_inc(act_ready, 1)
                else:
                    stt(dst, src, bias, r32(hi), ALU.add, ALU.subtract).then_inc(act_ready, 1)

            def add_squares():
                for k in range(1, KB):
                    t["sq"].add(2 if k == 1 else 1)
                    dve.wait_ge(sq_ready, t["sq"].now())
                    if k == 1:
                        tt(ss[:], sq[:, 0, :], sq[:, 1, :], ALU.add).then_inc(ss_added, 1)
                    else:
                        dve.wait_ge(ss_added, t["ss"].now())
                        tt(ss[:], ss[:], sq[:, k % 2, :], ALU.add).then_inc(ss_added, 1)
                    t["ss"].add()

            def invert(b):
                t["rt"].add()
                dve.wait_ge(rt_ready, t["rt"].now())
                dve.sem_inc(x_free[b], 1)
                link(dve.reciprocal(rinv[:], rinv[:]))
                t["aux"].add()

            def norm_split(hi, lo, gain, bias=None):
                add_squares()
                invert(1)
                dve.wait_ge(tile_done, t["tile"].now())

                def value(k):
                    dve.wait_ge(act_ready, t["op"].now())
                    signal(stt(sq[:, k % 2, :], xT[:, k, :], gain[:, k:k + 1], rinv[:], ALU.mult, ALU.mult),
                           val_ready, "val")

                value(0)
                for k in range(KB):
                    if k + 1 < KB:
                        value(k + 1)
                    low(lo[:, k, :], hi[:, k, :], sq[:, k % 2, :], None if bias is None else bias[:, k:k + 1])

            def norm_scale(gain):
                add_squares()
                invert(1)
                for k in range(KB):
                    stt(xT[:, k, :], xT[:, k, :], gain[:, k:k + 1], rinv[:], ALU.mult, ALU.mult).then_inc(x_ready, 1)
                    t["x"].add()

            dve.wait_ge(vec_landed, 16 * VECS)
            dve.tensor_copy(v3[0:XB, :].rearrange("b (r d) -> b r d", r=2),
                            dskip[:].unsqueeze(2).broadcast_to([XB, 2, HEAD_DIM])).then_inc(dskip_ready, 1)
            aux()
            dve.tensor_copy(v2T[:], X[0][:, P:2 * P]).then_inc(vec_ready, 1)
            dve.tensor_copy(v1T[:], X[0][:, 0:P].rearrange("p (j b) -> p j b", j=4))
            link(dve.tensor_copy(v3T[:, 0:VROWS], X[0][:, 2 * P:2 * P + VROWS]))
            dve.sem_inc(x_free[0], 1)
            for k in range(KB):
                tile()
                signal(dve.tensor_copy(xT[:, k, :], G[k % 4][:]), x_ready, "x", g_free[k % 4])
            add_squares()
            dve.wait_ge(c_ready, 1)

            def ada_sum(w, dst):
                link(ts(dst, w[:, 0, :], cact[:, 0:1], None, ALU.mult))
                for k in range(1, KB - 1):
                    link(stt(dst, w[:, k, :], cact[:, k:k + 1], dst, ALU.mult, ALU.add))
                stt(dst, w[:, KB - 1, :], cact[:, KB - 1:KB], dst, ALU.mult, ALU.add).then_inc(ada_acc, 1)

            def ada_unit(buf, acc):
                b = t["ada"].local % 2
                t["ada"].add()
                t[f"al{b}"].add(16)
                dve.wait_ge(ada_landed[b], t[f"al{b}"].now())
                dve.wait_ge(ada_used, t["ada"].now(-2))
                ada_sum(unit_view(buf[b]), acc[:, b, :])

            def unit_view(buf):
                return buf[:, :].rearrange("p (k n) -> p k n", k=KB)

            mine = [u for u in range(8) if u not in FIRST_ON_PE]
            for n, u in enumerate(mine):
                if n == 3:
                    invert(1)
                dve.wait_ge(first_landed[u], 16)
                if n >= 2:
                    dve.wait_ge(ada_used, mine[n - 2] + 1)
                ada_sum(unit_view(araw[u]), adacc[:, n % 2, :])
            t["ada"].add(8)
            dve.wait_ge(ada_used, 8)
            link(tt(modT[:, 0:2, :], X[3][:, 0:16].rearrange("p (j k) -> p j k", k=KB),
                    badaT[:, 0:16].rearrange("p (j k) -> p j k", k=KB), ALU.add))
            dve.sem_inc(x_free[3], 1)
            link(stt(coef[:], modT[:, 1, :], 1.0, ln1T, ALU.add, ALU.mult))
            t["hi"].add()
            dve.wait_ge(hi_split, t["hi"].now())
            n0 = KB * HEADS
            tt(wlo[0][:, 0:n0], raw[0][:, 0:n0], r32(whi[0][:, 0:n0]), ALU.subtract).then_inc(lo_split, 1)
            slot[0] = 1

            def value(k):
                if k >= 2:
                    dve.wait_ge(act_ready, t["op"].now())
                signal(stt(sq[:, k % 2, :], xT[:, k, :], coef[:, k:k + 1], rinv[:], ALU.mult, ALU.mult),
                       val_ready, "val")

            value(0)
            for k in range(KB):
                if k + 1 < KB:
                    value(k + 1)
                low(alo[:, k, :], ahi[:, k, :], sq[:, k % 2, :], modT[:, 0, k:k + 1])
            link(dve.memset(pacc[:], 0.0))
            link(dve.memset(pre[:, :, 0:3], 0.0))

            unit()
            tile()
            dve.wait_ge(vec_landed, 16 * VECS)
            heads = lambda kind: dts[:, kind]
            over = lambda j: dtw[:, j, :].unsqueeze(1).broadcast_to([P, TB, HEADS])
            tt(heads(TMP), G[0][:, 0:P].rearrange("p (c h) -> p c h", c=TB), over(0), ALU.add).then_inc(prep_v, 1)
            dve.wait_ge(prep_v, 1)
            dve.sem_inc(g_free[0], 1)
            dve.wait_ge(prep_a, 1)
            ts(heads(AC), heads(DT), 1.0, None, ALU.add).then_inc(prep_v, 1)
            dve.wait_ge(prep_v, 2)
            link(ts(heads(TOEND), heads(AC), -1.0, None, ALU.add))
            link(ts(heads(EEND), heads(TOEND), 0.0, None, ALU.is_equal))
            link(tt(heads(TOEND), heads(TOEND), heads(EEND), ALU.add))
            link(dve.reciprocal(heads(TOEND), heads(TOEND)))
            link(tt(heads(TOEND), heads(TOEND), heads(DT), ALU.mult))
            dve.wait_ge(prep_a, 2)
            link(tt(heads(TOEND), heads(TOEND), heads(EAC), ALU.mult))
            link(tt(heads(EEND), heads(EEND), heads(DT), ALU.mult))
            link(tt(heads(TOEND), heads(TOEND), heads(EEND), ALU.add))
            link(stt(heads(DT), heads(TMP), 0.0, heads(TOEND), ALU.max, ALU.add))
            stt(heads(TMP), heads(DT), -1.0, over(1), ALU.mult, ALU.mult).then_inc(prep_v, 1)

            def convs(first, blks, bank):
                steps = []
                for m, blk in zip((first, first + 1), blks):
                    t["pre"].add()
                    seen = t["pre"].local

                    def step(j, m=m, blk=blk, seen=seen):
                        if j == 0:
                            dve.wait_ge(pre_ready, t["pre"].now(seen - t["pre"].local))
                            dve.sem_inc(g_free[bank + m - first], 1)
                        ins = stt(cv[:, m, :], pre[:, m, j:j + T], v1T[:, j, bass.ds(blk, 1)], cv[:, m, :],
                                  ALU.mult, ALU.add)
                        if j < 2:
                            link(ins)
                        else:
                            ins.then_inc(cv_ready, 1)

                    steps += [lambda j=j, step=step: step(j) for j in range(3)]
                return steps

            def group_heads(kind, c0, c1, g):
                v = dts[:, kind, c0:c1, bass.ds(g * RH, RH)]
                return v.unsqueeze(3).broadcast_to([P, c1 - c0, RH, HEAD_DIM])

            def by_head(ap):
                return ap.rearrange("p c (r d) -> p c r d", r=RH)

            def two(bank):
                return bank[:].rearrange("p (c r d) -> p c r d", c=2, r=RH)

            def scan_turn(g, gemm, ssd, outp):
                q = g - 1
                steps = []
                if outp:
                    t["sq"].add(2)
                    dve.wait_ge(sq_ready, t["sq"].now())
                    signal(tt(ss[:], sq[:, 0, :], sq[:, 1, :], ALU.add), ss_added, "ss")
                if gemm:
                    s = unit()
                    t["tile"].add(2)
                    steps = convs(0, (2 * g, 2 * g + 1), 2 * s)
                    for step in steps[0:3]:
                        step()
                if outp:
                    invert(2)
                    for b in range(2):
                        signal(stt(sq[:, b, :], yf[:, b, :], v3T[:, bass.ds(normw0 + 2 * (g - 2) + b, 1)], rinv[:],
                                   ALU.mult, ALU.mult), val_ready, "val")
                for step in steps[3:6]:
                    step()
                if outp:
                    for b in range(2):
                        low(ylo[:, b, :], yhi[:, b, :], sq[:, b, :])
                if gemm:
                    s = unit()
                    t["tile"].add(2)
                if ssd:
                    for half in range(2):
                        aux()
                        tt(by_head(xdt[:, 2 * half:2 * half + 2, :]), two(X[half]),
                           group_heads(DT, 2 * half, 2 * half + 2, q), ALU.mult).then_inc(x_free[half], 1)
                    t["aux"].add()
                    aux()
                    link(tt(sm[:], X[3][:].rearrange("p (c n) -> p c n", c=TB),
                            triu[:].unsqueeze(1).broadcast_to([P, TB, P]), ALU.mult))
                    dve.sem_inc(x_free[3], 1)
                    t["exp"].add()
                    for r in range(RH):
                        dve.wait_ge(exp_ready, t["exp"].now(r))
                        if r == 0:
                            tt(by_head(xw[:]), by_head(xdt[:]), group_heads(TOEND, 0, TB, q), ALU.mult)\
                                .then_inc(xw_ready, 1)
                        tt(seg[:, r, :], seg[:, r, :], sm[:].rearrange("p c n -> p (c n)"), ALU.mult)\
                            .then_inc(m_ready, 1)
                    t["exp"].add(RH - 1)
                steps = convs(2, (XB + g, XB + GROUPS + g), 2 * s) if gemm else []
                if steps:
                    steps.pop(0)()
                    steps.pop(2)()
                if outp:
                    so = unit()
                    for m in range(KB):
                        tile()
                        tt(pacc[:, m, :], pacc[:, m, :], G[(2 * so + m) % 4][:], ALU.add)\
                            .then_inc(g_free[(2 * so + m) % 4], 1)
                        if steps:
                            steps.pop(0)()
                for step in steps:
                    step()
                if gemm:
                    unit()
                if ssd:
                    t["aux"].add()
                    aux()
                    link(dve.tensor_copy(states[:, 0, :], X[2][:, 0:GW]))
                    for c in (1, 2):
                        link(tt(states[:, c, :].rearrange("p (r d) -> p r d", r=RH),
                                states[:, c - 1, :].rearrange("p (r d) -> p r d", r=RH),
                                dts[:, EEND, c, bass.ds(q * RH, RH)].unsqueeze(2).broadcast_to([P, RH, HEAD_DIM]),
                                ALU.mult))
                        src = X[2][:, GW:2 * GW] if c == 1 else X[3][:, 0:GW]
                        ins = tt(states[:, c, :], states[:, c, :], src, ALU.add)
                        if c == 1:
                            link(ins)
                            dve.sem_inc(x_free[2], 1)
                        else:
                            signal(ins, st_ready, "st", x_free[3])
                if ssd:
                    aux()
                    link(tt(by_head(ytok[:, 1:3, :]), two(X[2]), group_heads(EAC, 1, 3, q), ALU.mult))
                    dve.sem_inc(x_free[2], 1)
                    link(tt(by_head(ytok[:, 3:4, :]), X[3][:, 0:GW].rearrange("p (c r d) -> p c r d", c=1, r=RH),
                            group_heads(EAC, 3, 4, q), ALU.mult))
                    dve.sem_inc(x_free[3], 1)
                    dve.tensor_copy(ytok[:, 0, :], X[0][:, 0:GW])
                    tt(ytok[:, 1, :], ytok[:, 1, :], X[0][:, GW:2 * GW], ALU.add).then_inc(x_free[0], 1)
                    signal(tt(ytok[:, 2:4, :], ytok[:, 2:4, :], X[1][:].rearrange("p (c n) -> p c n", c=2), ALU.add),
                           ytok_ready, "yt", x_free[1])
                    for b in range(2):
                        aux()
                        link(stt(yf[:, b, :], xf[:, b, :], v3T[:, bass.ds(dskip0 + 2 * q + b, 1)], X[b][:],
                                 ALU.mult, ALU.add))
                        dve.sem_inc(x_free[b], 1)
                        tt(yf[:, b, :], yf[:, b, :], zs[:, b, :], ALU.mult).then_inc(yf_ready, 1)
                if gemm:
                    t["tile"].add(2)

            scan_turn(0, True, False, False)
            aux()
            link(dve.tensor_copy(heads(AC), X[0][:, 0:P].rearrange("p (c h) -> p c h", c=TB)))
            aux()
            tt(heads(TOEND), X[1][:, 0:P].rearrange("p (c h) -> p c h", c=TB), heads(AC), ALU.subtract)\
                .then_inc(prep_v, 1)
            t["aux"].add()
            dve.wait_ge(prep_a, 3)
            for b in range(3):
                dve.sem_inc(x_free[b], 1)
            scan_turn(1, True, True, False)
            with turns(dve, GROUPS - 2, t, {"hi": 4, "tile": 14, "aux": 10, "sq": 2, "ss": 1, "rt": 1, "val": 2,
                                            "vhi": 2, "op": 2, "pre": 4, "exp": 4, "st": 1, "yt": 1, "step": 18}) as i:
                scan_turn(i + 2, True, True, True)
            scan_turn(GROUPS, False, True, True)
            scan_turn(GROUPS + 1, False, False, True)

            def gate_used(s, m):
                t["tile"].add()
                t["sg"].add()
                dve.wait_ge(sg_ready, t["sg"].now())
                dve.sem_inc(g_free[2 * s + m], 1)

            dve.sem_inc(sg_used, 1)
            with turns(dve, 2, t, {"hi": 2, "tile": 4, "sg": 4, "ada": 2, "al0": 16, "al1": 16, "step": 14}) as i:
                for u in range(2):
                    s = unit()
                    ada_unit(braw, badacc)
                    for m in range(2):
                        gate_used(s, m)
                        dst = pacc[:, bass.ds(4 * i + 2 * u + m, 1), :]
                        tt(dst, dst, sq[:, m, :].unsqueeze(1), ALU.mult).then_inc(sg_used, 1)
            link(dve.memset(pb[:, :, 0:2], 0.0))
            t["used"].add(9)
            with turns(dve, 4, t, {"hi": 2, "tile": 4, "sg": 2, "ada": 2, "al0": 16, "al1": 16, "step": 20,
                                   "used": 2}) as i:
                s = unit()
                ada_unit(braw, badacc)
                for m in range(2):
                    gate_used(s, m)
                s = unit()
                ada_unit(braw, badacc)
                for m in range(2):
                    tile()
                    signal(tt(pb[:, m, 2:2 + T], G[2 * s + m][:], ccs[:, m, :], ALU.mult), sg_used, "used",
                           g_free[2 * s + m])
                    dst = qc[:, bass.ds(2 * i + m, 1), :]
                    link(ts(dst, pb[:, m, 2:2 + T].unsqueeze(1), v2T[:, bass.ds(convw0 + 2 * KB + 2 * i + m, 1)], None,
                            ALU.mult))
                    for j in (1, 0):
                        link(stt(dst, pb[:, m, j:j + T].unsqueeze(1), v2T[:, bass.ds(convw0 + j * KB + 2 * i + m, 1)],
                                 dst, ALU.mult, ALU.add))
            with turns(dve, 2, t, {"hi": 2, "tile": 4, "val": 4, "vhi": 4, "op": 4, "ada": 2, "al0": 16, "al1": 16,
                                   "step": 14}) as i:
                for u in range(2):
                    s = unit()
                    ada_unit(braw, badacc)
                    for m in range(2):
                        tile()
                        k = bass.ds(4 * i + 2 * u + m, 1)
                        signal(tt(sq[:, m, :].unsqueeze(1), G[2 * s + m][:].unsqueeze(1), qc[:, k, :], ALU.mult),
                               val_ready, "val", g_free[2 * s + m])
                        low(blo[:, k, :], bhi[:, k, :], sq[:, m, :].unsqueeze(1))
            dve.wait_ge(ada_used, 24)
            link(tt(modT[:, 2:6, :], X[3][:, 16:48].rearrange("p (j k) -> p j k", k=KB),
                    badaT[:, 16:48].rearrange("p (j k) -> p j k", k=KB), ALU.add))
            dve.sem_inc(x_free[3], 1)
            link(stt(coef[:], modT[:, 4, :], 1.0, ln2T, ALU.add, ALU.mult))
            with turns(dve, 4, t, {"hi": 2, "tile": 4, "sg": 2, "val": 2, "vhi": 2, "op": 2, "step": 2}) as i:
                s = unit()
                for m in range(2):
                    gate_used(s, m)
                s = unit()
                for m in range(2):
                    tile()
                    k = bass.ds(2 * i + m, 1)
                    link(tt(sq[:, m, :], G[2 * s + m][:], ccs[:, m, :], ALU.mult))
                    dve.sem_inc(g_free[2 * s + m], 1)
                    signal(tt(sq[:, m, :].unsqueeze(1), sq[:, m, :].unsqueeze(1), pacc[:, k, :], ALU.add),
                           val_ready, "val")
                    low(clo[:, k, :], chi[:, k, :], sq[:, m, :].unsqueeze(1))

            def residual(s, m, k, gain):
                tile()
                dst = xT[:, k, :]
                src = G[2 * s + m][:].unsqueeze(1)
                signal(stt(dst, src, gain, dst, ALU.mult, ALU.add), x_ready, "x", g_free[2 * s + m])

            with turns(dve, 2, t, {"hi": 2, "tile": 4, "x": 4}) as i:
                for u in range(2):
                    s = unit()
                    for m in range(2):
                        residual(s, m, bass.ds(4 * i + 2 * u + m, 1), modT[:, 2, bass.ds(4 * i + 2 * u + m, 1)])
            norm_split(ahi, alo, coef, modT[:, 3, :])
            with turns(dve, 4, t, {"hi": 8, "tile": 16, "sg": 8, "val": 8, "vhi": 8, "op": 8, "x": 8}):
                for u in range(4):
                    s = unit()
                    for m in range(2):
                        gate_used(s, m)
                        signal(tt(sq[:, m, :], gs[:, m, :], gs[:, m, :], ALU.mult), val_ready, "val")
                        low(hlo[:, 2 * u + m, :], hhi[:, 2 * u + m, :], sq[:, m, :])
                for u in range(4):
                    s = unit()
                    for m in range(2):
                        residual(s, m, slice(2 * u + m, 2 * u + m + 1), modT[:, 5, 2 * u + m:2 * u + m + 1])

            def swiglu(gain, last=False, twice=False):
                dve.wait_ge(tile_done, t["tile"].now())
                for k in range(KB):
                    t["vhi"].add()
                    t["op"].add()
                    dve.wait_ge(val_hi, t["vhi"].now())
                    stt(alo[:, k, :], xT[:, k, :], gain[:, k:k + 1], r32(ahi[:, k, :]), ALU.mult, ALU.subtract)\
                        .then_inc(act_ready, 1)
                s0 = unit()
                for k in range(1, KB):
                    t["sq"].add(2 if k == 1 else 1)
                    dve.wait_ge(sq_ready, t["sq"].now())
                    if k > 1:
                        dve.wait_ge(ss_added, t["ss"].now())
                    if twice:
                        tt(rr[:], gs[:, 0, :] if k == 1 else rr[:], gs[:, k % 2, :], ALU.add)
                    tt(ss[:], sq[:, 0, :] if k == 1 else ss[:], sq[:, k % 2, :], ALU.add).then_inc(ss_added, 1)
                    t["ss"].add()
                s1 = unit()
                invert(1)
                if twice:
                    aux()
                    link(stt(rr[:], X[0][:], 1.0 / D, rinv[:], ALU.mult, ALU.mult))
                    dve.sem_inc(x_free[0], 1)
                    tt(rr[:], rr[:], rinv[:], ALU.mult).then_inc(fx_ready, 1)
                    t["rt"].add()
                    dve.wait_ge(rt_ready, t["rt"].now())
                    link(dve.reciprocal(rr[:], rr[:]))
                    link(tt(rr[:], rr[:], rinv[:], ALU.mult))
                    norms = rr
                else:
                    norms = rinv

                def slab(pairs, last=False, first=False):
                    for u in range(pairs):
                        s = unit() if u or not first else s0
                        for m in range(2):
                            tile()
                            signal(tt(gs[:, m, :], G[2 * s + m][:], norms[:], ALU.mult), gr_ready, "gr",
                                   g_free[2 * s + m])
                        s = unit() if u or not first else s1
                        for m in range(2):
                            tile()
                            t["sg"].add()
                            dve.wait_ge(sg_ready, t["sg"].now())
                            link(tt(sq[:, m, :], gs[:, m, :], G[2 * s + m][:], ALU.mult))
                            dve.sem_inc(g_free[2 * s + m], 1)
                            tt(sq[:, m, :], sq[:, m, :], norms[:], ALU.mult).then_inc(val_ready, 1)
                            t["val"].add()
                            if twice and u == 0 and first and m == 1:
                                for k in range(KB):
                                    stt(xT[:, k, :], xT[:, k, :], finalT[:, k:k + 1], rinv[:], ALU.mult, ALU.mult)\
                                        .then_inc(x_ready, 1)
                                    t["x"].add()
                            low(hlo[:, 2 * u + m, :], hhi[:, 2 * u + m, :], sq[:, m, :])
                    for u in range(4):
                        s = unit(last and u == 3)
                        for m in range(2):
                            residual(s, m, slice(2 * u + m, 2 * u + m + 1), 0.5)

                slab(4, first=True)
                slab(4)
                slab(3, last)

            link(tt(gf[:], gf1T, finalT, ALU.mult))
            dve.sem_inc(gf_ready, 1)
            swiglu(gf, twice=True)

            norm_split(ahi, alo, gmixT)

            def rope(dst, src, tmp, tab, half, w):
                heads = src.shape[2]
                h = w // 2

                def row(j, lo, hi):
                    return tab[:, j, 2 * half:2 * half + 2, lo:hi].unsqueeze(2).broadcast_to([P, 2, heads, hi - lo])

                tt(dst, src, row(0, 0, w), ALU.mult)
                tt(tmp[:, :, :, 0:h], src[:, :, :, h:w], row(1, 0, h), ALU.mult)
                link(tt(tmp[:, :, :, h:w], src[:, :, :, 0:h], row(1, h, w), ALU.mult))
                link(tt(dst, dst, tmp, ALU.add))

            def tmp4(heads, w):
                return rtmp[:, 0:2 * heads * w].rearrange("p (b h d) -> p b h d", b=2, h=heads)

            s = unit()
            dve.wait_ge(tab_landed, 16 * 5)
            link(dve.memset(score[:], 0.0))
            link(dve.memset(biasM[:, 0:T - P], 0.0))
            link(dve.tensor_copy(biasM[:, T - P:T], nmask[:]))
            link(dve.tensor_copy(bias[:, 0:P], nmask[:]))
            for half in range(2):
                tile()
                b2 = slice(2 * half, 2 * half + 2)
                src = G[2 * s + half][:].rearrange("p (b n) -> p b n", b=2)
                for dst, at in ((kk, 0), (qtok, M_KI)):
                    rope(dst[:, b2, 0:HD].unsqueeze(2), src[:, :, at:at + HD].unsqueeze(2), tmp4(1, HD), tab64, half, HD)
                    link(dve.tensor_copy(dst[:, b2, HD:2 * HD], dst[:, b2, 0:HD]))
                rope(krt[:, b2, :].unsqueeze(2), src[:, :, M_KR:M_KR + ROPE].unsqueeze(2), tmp4(1, ROPE), tab32, half,
                     ROPE)
                link(dve.tensor_copy(va[:, b2, :], src[:, :, M_VA:M_VA + HD]))
                signal(ts(wix[:, b2, :], src[:, :, M_WI:M_WI + IDX_HEADS], 1.0 / 32.0, None, ALU.mult),
                       k_ready, "k", g_free[2 * s + half])
            t["aux"].add(2)

            def rope_unit():
                s = unit()
                if t["aux"].now():
                    dve.wait_ge(aux_done, t["aux"].now())
                for half in range(2):
                    tile()
                    b2 = slice(2 * half, 2 * half + 2)
                    rope(qtok[:, b2, 0:UC].rearrange("p b (h d) -> p b h d", h=4),
                         G[2 * s + half][:].rearrange("p (b h d) -> p b h d", b=2, h=4), tmp4(4, HD), tab64, half, HD)
                    if half == 0:
                        dve.sem_inc(g_free[2 * s], 1)
                dve.sem_inc(g_free[2 * s + 1], 1)
                dve.sem_inc(k_ready, 1)
                t["k"].add()

            def index_sums(u):
                for n in range(12):
                    h, q = 4 * u + n // 3, n % 3 + 1
                    t["aux"].add()
                    t["rl"].add()
                    dve.wait_ge(rl_ready, t["rl"].now())
                    dve.sem_inc(x_free[2 + n % 2], 1)
                    w = (q + 1) * P
                    dst = score[:, SOFF[q]:SOFF[q] + w]
                    if n >= 3:
                        dve.wait_ge(rl_used, t["rl"].now(-3))
                    stt(dst, pT[:, n % 2, 0:w], wix[:, q, h:h + 1], dst, ALU.mult, ALU.add).then_inc(rl_used, 1)

            def search():
                dve.wait_ge(rl_used, t["rl"].now())
                for q in range(1, TB):
                    w = (q + 1) * P
                    mine = score[:, SOFF[q]:SOFF[q] + w]
                    link(tt(mine[:, q * P:w], mine[:, q * P:w], nmask[:], ALU.add))
                    for _ in range(TOPK // 8):
                        link(dve.max(m8[:], mine))
                        link(dve.match_replace(mine, m8[:], mine, TAKEN))
                        yield
                    link(ts(bias[:, BOFF[q]:BOFF[q] + w], mine, TAKEN / 2, NEG, ALU.is_gt, ALU.mult))

            rounds = search()

            def some_rounds(n):
                for _ in range(n):
                    next(rounds, None)

            for u in range(4):
                rope_unit()
                if u:
                    index_sums(u - 1)
                t["aux"].add(2)
            for u in range(2):
                rope_unit()
                if u == 0:
                    index_sums(3)
                t["aux"].add(2)
                some_rounds(4)
            for u in range(3):
                unit()
                t["tile"].add(2)
                some_rounds(6)
            dve.wait_ge(lat_ready, 1)
            link(dve.reciprocal(sm1[:, 0:8], sm1[:, 0:8]))
            for b in range(TB):
                ts(lat[:, b, 0:384], lat[:, b, 0:384], sm1[:, b:b + 1], None, ALU.mult)
                last = ts(lat[:, b, 384:640], lat[:, b, 384:640], sm1[:, 4 + b:5 + b], None, ALU.mult)
            last.then_inc(lat_done, 1)
            for j in range(LATB):
                t["vhi"].add()
                t["aux"].add()
                dve.wait_ge(val_hi, t["vhi"].now())
                link(stt(llo[:, j, :], X[j % 2][:], v3T[:, latg0 + j:latg0 + j + 1], r32(lhi[:, j, :]), ALU.mult,
                         ALU.subtract))
                t["op"].add()
                dve.sem_inc(act_ready, 1)
                dve.sem_inc(x_free[j % 2], 1)

            def heads96(b):
                return qtok[:, b, :].rearrange("p (h d) -> p h d", h=4)

            def rope96(dst, src, b):
                h = ROPE // 2
                tmp = rtmp[:, 0:4 * ROPE].rearrange("p (h d) -> p h d", h=4)

                def row(j, lo, hi):
                    return tab32[:, j, b, lo:hi].unsqueeze(1).broadcast_to([P, 4, hi - lo])

                tt(dst, src, row(0, 0, ROPE), ALU.mult)
                tt(tmp[:, :, 0:h], src[:, :, h:ROPE], row(1, 0, h), ALU.mult)
                link(tt(tmp[:, :, h:ROPE], src[:, :, 0:h], row(1, h, ROPE), ALU.mult))
                link(tt(dst, dst, tmp, ALU.add))

            for u in range(2):
                s = unit()
                dve.wait_ge(aux_done, t["aux"].now())
                for b in range(TB):
                    tile()
                    src = G[2 * s + b % 2][:, 0:4 * QH].rearrange("p (h d) -> p h d", h=4)
                    link(dve.tensor_copy(heads96(b)[:, :, 0:HD], src[:, :, 0:HD]))
                    rope96(heads96(b)[:, :, HD:QH], src[:, :, HD:QH], b)
                    dve.sem_inc(g_free[2 * s + b % 2], 1)
                dve.sem_inc(k_ready, 1)
                t["aux"].add(4)
                some_rounds(7)
            for u in range(2):
                s = unit()
                dve.wait_ge(aux_done, t["aux"].now())
                for b in range(TB):
                    tile()
                    src = G[2 * s + b % 2][:].rearrange("p (h d) -> p h d", h=4)
                    dve.tensor_copy(heads96(b)[:, :, 0:HD], src[:, :, 0:HD])
                    dve.tensor_copy(heads96(b)[:, :, HD:QH], krt[:, b, :].unsqueeze(1).broadcast_to([P, 4, ROPE]))
                    link(dve.tensor_copy(vt[:, b, 4 * HD * u:4 * HD * (u + 1)].rearrange("p (h d) -> p h d", h=4),
                                         src[:, :, HD:2 * HD]))
                    dve.sem_inc(g_free[2 * s + b % 2], 1)
                dve.sem_inc(k_ready, 1)
                t["aux"].add(4)
                some_rounds(7)
            some_rounds(100)

            for latent in range(2):
                scale = QH ** -0.5 if latent else HD ** -0.5
                with turns(dve, NH // 2, t, {"aux": 24, "lg": 8, "pr": 8, "step": 24}) as i:
                    for n in range(11):
                        if n < 8:
                            q = n % TB
                            w = (q + 1) * P
                            aux()
                            mask = biasM[:, T - w:T] if latent else bias[:, BOFF[q]:BOFF[q] + w]
                            link(stt(pw[n % 4][:, 0:w], X[n % 2][:, 0:w], scale, mask, ALU.mult, ALU.add))
                            dve.sem_inc(x_free[n % 2], 1)
                            t["lg"].add()
                            dve.tensor_reduce(sm1[:, n % 4:n % 4 + 1], pw[n % 4][:, 0:w], AX_X, ALU.max, negate=True)\
                                .then_inc(lg_ready, 1)
                        if 2 <= n < 10:
                            t["aux"].add()
                        if n >= 3:
                            m = (n - 3) % 4
                            t["pr"].add()
                            dve.wait_ge(p_ready, t["pr"].now())
                            link(dve.reciprocal(sm1[:, 12 + m:13 + m], sm1[:, 8 + m:9 + m]))
                            aux()
                            q = (n - 3) % TB
                            at = latent * T + (2 * i + (n - 3) // TB) * HD
                            link(ts(otok[:, q, bass.ds(at, HD)], X[3][:, 0:HD], sm1[:, 12 + m:13 + m], None, ALU.mult))
                            dve.sem_inc(x_free[3], 1)
            dve.sem_inc(o_ready, 1)
            for k in range(KB):
                t["vhi"].add()
                t["aux"].add()
                dve.wait_ge(val_hi, t["vhi"].now())
                link(tt(alo[:, k, :], X[k % 4][:], r32(ahi[:, k, :]), ALU.subtract))
                t["op"].add()
                dve.sem_inc(act_ready, 1)
                dve.sem_inc(x_free[k % 4], 1)
            for u in range(4):
                s = unit()
                for m in range(2):
                    residual(s, m, slice(2 * u + m, 2 * u + m + 1), 1.0)
            swiglu(gf2T, last=True)
            norm_scale(gfinT)
            for n in range(2 * TB):
                aux()
                bank = 2 * ((n // 2) % 2) + n % 2
                signal(dve.tensor_copy(xout[:, n // 2, (n % 2) * T:(n % 2 + 1) * T], X[bank][:]), o_copied, "oc",
                       x_free[bank])


INPUTS = ("x", "c", "w_ada", "b_ada", "ln1", "ln2", "w_in", "conv_w", "ssm_conv_w", "ssm_conv_b", "dt_bias",
          "a_log", "d_skip", "ssm_norm_w", "w_conv_out", "w_ssm_out", "w_o", "w_up", "w_down", "final_norm",
          "g_ffn1_2", "w1_gate_2", "w1_up_2", "w1_down_2", "g_mix_2", "w_in_2", "g_q_lat_2", "g_kv_lat_2",
          "w_uq_2", "w_ukv_2", "w_out_2", "g_ffn2_2", "w2_gate_2", "w2_up_2", "w2_down_2", "g_final_2")


def constants():
    def rotary(dim):
        pos = np.arange(T, dtype=np.float32)
        inv = np.float32(10000.0) ** (-np.arange(0, dim, 2, dtype=np.float32) / np.float32(dim))
        ang = pos[:, None] * inv[None, :].astype(np.float32)
        cos, sin = np.cos(ang).astype(np.float32), np.sin(ang).astype(np.float32)
        return np.concatenate([cos, cos], 1), np.concatenate([-sin, sin], 1)

    cos64, sin64 = rotary(HD)
    cos32, sin32 = rotary(ROPE)
    row = np.arange(P)
    return {
        "ident": np.eye(P, dtype=np.float32),
        "triu": (row[:, None] <= row[None, :]).astype(np.float32),
        "nmask": np.where(row[None, :] <= row[:, None], 0.0, NEG).astype(np.float32),
        "cos64": cos64, "sin64": sin64, "cos32": cos32, "sin32": sin32,
    }


def kernel(**inputs):
    import concourse.bacc as bacc
    from concourse.bass_utils import run_bass_kernel_spmd

    nc = bacc.Bacc("TRN2", target_bir_lowering=False, num_devices=1)
    arrays, aps = {}, {}
    given = {name: inputs[name] for name in INPUTS}
    for name, value in {**given, **constants()}.items():
        value = np.ascontiguousarray(value)
        arrays[f"in_{name}"] = value
        aps[name] = nc.dram_tensor(f"in_{name}", value.shape, mybir.dt.from_np(value.dtype), kind="ExternalInput").ap()
    out = nc.dram_tensor("out_x", (1, T, D), F32, kind="ExternalOutput").ap()
    build(nc, aps, out)
    result = run_bass_kernel_spmd(nc, [arrays], core_ids=[0])
    return result.results[0]["out_x"]
```
